# Optimizing a Trainium2 kernel written in Bass

```python
import math
import jax, jax.numpy as jnp
from jax import lax
import numpy as np

D_MODEL = 1024
BATCH = 1
SEQ = 256
DEPTH = 1
DEC_BATCH = 1
DEC_SEQ = 64
PAST_LEN = 256

CHUNK = 64
Q_BLOCK = 128
A_HEADS = 8
A_DH = 64
A_DV = 2 * A_DH
B_HEADS = 16
B_DH = 64
ROPE_THETA = 500000.0
ROPE_DIMS = A_DH // 4
N_GROUPS = 4
EXP_PER_GROUP = 8
N_EXPERTS = N_GROUPS * EXP_PER_GROUP
TOP_K = 2
D_EXPERT = 256
EPS = 1e-6
NEG_INF = -1e30
A_QW = 2 * A_HEADS * A_DH
A_KW = 2 * A_HEADS * A_DH
A_VW = A_HEADS * A_DV
B_W = B_HEADS * B_DH
IN_COLS = A_QW + A_KW + A_VW + 3 * B_W + 2 * D_MODEL

kernel_name = 'hybrid_diffattn_stickbreak_hmoe_stream_step'

def _rmsnorm(x, g):
    xf = x.astype(jnp.float32)
    y = xf * lax.rsqrt(jnp.mean(xf * xf, axis=-1, keepdims=True) + EPS)
    return (y * g.astype(jnp.float32)).astype(x.dtype)

def _partial_rope(x, pos):
    half = ROPE_DIMS // 2
    inv_freq = jnp.exp(-math.log(ROPE_THETA) * 2.0 * jnp.arange(half, dtype=jnp.float32) / ROPE_DIMS)
    ang = pos.astype(jnp.float32)[:, None] * inv_freq[None, :]
    cos = jnp.cos(ang)[None, :, None, :]
    sin = jnp.sin(ang)[None, :, None, :]
    xf = x.astype(jnp.float32)
    x1 = xf[..., :half]
    x2 = xf[..., half:ROPE_DIMS]
    out = jnp.concatenate([x1 * cos - x2 * sin, x2 * cos + x1 * sin, xf[..., ROPE_DIMS:]], axis=-1)
    return out.astype(x.dtype)

def _diff_attention(q, k, v, q_off, lam, lam_init, subln_g):
    bsz, tq = q.shape[0], q.shape[1]
    tk = k.shape[1]
    qb = Q_BLOCK if tq % Q_BLOCK == 0 else tq
    qf = q.astype(jnp.float32) * (1.0 / math.sqrt(A_DH))
    kf = k.astype(jnp.float32)
    vf = v.astype(jnp.float32)
    outs = []
    for j in range(tq // qb):
        t0 = q_off + j * qb
        kend = min(tk, ((t0 + qb - 1) // CHUNK + 1) * CHUNK)
        s = jnp.einsum('bqhd,bkhd->bhqk', qf[:, j * qb:(j + 1) * qb], kf[:, :kend])
        qpos = t0 + jnp.arange(qb)
        kpos = jnp.arange(kend)
        mask = (kpos[None, :] // CHUNK) <= (qpos[:, None] // CHUNK)
        p = jax.nn.softmax(jnp.where(mask, s, NEG_INF), axis=-1)
        p = p.reshape(bsz, A_HEADS, 2, qb, kend)
        a = p[:, :, 0] - lam * p[:, :, 1]
        outs.append(jnp.einsum('bhqk,bkhd->bqhd', a, vf[:, :kend]))
    o = jnp.concatenate(outs, axis=1)
    return _rmsnorm(o, subln_g) * (1.0 - lam_init)

def _stick_breaking(q, k, v, q_off):
    tq = q.shape[1]
    tk = k.shape[1]
    qb = Q_BLOCK if tq % Q_BLOCK == 0 else tq
    qf = q.astype(jnp.float32) * (1.0 / math.sqrt(B_DH))
    kf = k.astype(jnp.float32)
    vf = v.astype(jnp.float32)
    outs = []
    for j in range(tq // qb):
        t0 = q_off + j * qb
        kend = max(1, min(tk, t0 + qb - 1))
        z = jnp.einsum('bqhd,bkhd->bhqk', qf[:, j * qb:(j + 1) * qb], kf[:, :kend])
        qpos = t0 + jnp.arange(qb)
        kpos = jnp.arange(kend)
        mask = kpos[None, :] < qpos[:, None]
        log_beta = jax.nn.log_sigmoid(z)
        log_rest = jnp.where(mask, jax.nn.log_sigmoid(-z), 0.0)
        after = lax.cumsum(log_rest, axis=3, reverse=True) - log_rest
        w = jnp.where(mask, jnp.exp(log_beta + after), 0.0)
        outs.append(jnp.einsum('bhqk,bkhd->bqhd', w, vf[:, :kend]))
    return jnp.concatenate(outs, axis=1)

def _hier_moe(h, w_rg, b_rg, w_re, b_re, w1, w3, w2):
    bsz, t, d = h.shape
    hf = h.reshape(bsz * t, d)
    n = hf.shape[0]
    rows = jnp.arange(n)
    pg = jax.nn.softmax((hf @ w_rg + b_rg).astype(jnp.float32), axis=-1)
    g_sel = jnp.argmax(pg, axis=-1)
    pg_sel = pg[rows, g_sel][:, None]
    le = (hf @ w_re + b_re).astype(jnp.float32).reshape(n, N_GROUPS, EXP_PER_GROUP)
    pe = jax.nn.softmax(le[rows, g_sel], axis=-1)
    top_w, top_i = lax.top_k(pe, TOP_K)
    top_w = top_w / jnp.sum(top_w, axis=-1, keepdims=True) * pg_sel
    eid = g_sel[:, None] * EXP_PER_GROUP + top_i
    gate = jnp.sum(jax.nn.one_hot(eid, N_EXPERTS, dtype=jnp.float32) * top_w[..., None], axis=1)
    hid = jax.nn.silu(jnp.einsum('nd,edf->nef', hf, w1)) * jnp.einsum('nd,edf->nef', hf, w3)
    hid = hid * gate[..., None].astype(hid.dtype)
    y = jnp.einsum('nef,efd->nd', hid, w2)
    return y.reshape(bsz, t, d)

def _layer(x, c, past, lam_init, norm1_g, norm2_g, w_ada, b_ada, w_in, a_qnorm_g, a_knorm_g,
           a_lam_q1, a_lam_k1, a_lam_q2, a_lam_k2, a_subln_g, w_oa, w_ob, w_out,
           w_rg, b_rg, w_re, b_re, w1, w3, w2):
    bsz, t, _ = x.shape
    q_off = 0 if past is None else past[0].shape[1]
    pos = q_off + jnp.arange(t)
    mod = jax.nn.silu(c) @ w_ada + b_ada
    sh1, sc1, g1, sh2, sc2, g2 = [m[:, None, :] for m in jnp.split(mod, 6, axis=-1)]
    h = _rmsnorm(x, norm1_g) * (1.0 + sc1) + sh1
    proj = h @ w_in
    o1 = A_QW
    o2 = o1 + A_KW
    o3 = o2 + A_VW
    o4 = o3 + B_W
    o5 = o4 + B_W
    o6 = o5 + B_W
    o7 = o6 + D_MODEL
    qa = proj[..., :o1].reshape(bsz, t, 2 * A_HEADS, A_DH)
    ka = proj[..., o1:o2].reshape(bsz, t, 2 * A_HEADS, A_DH)
    va = proj[..., o2:o3].reshape(bsz, t, A_HEADS, A_DV)
    qs = proj[..., o3:o4].reshape(bsz, t, B_HEADS, B_DH)
    ks = proj[..., o4:o5].reshape(bsz, t, B_HEADS, B_DH)
    vs = proj[..., o5:o6].reshape(bsz, t, B_HEADS, B_DH)
    gate_a = jax.nn.sigmoid(proj[..., o6:o7])
    gate_b = jax.nn.sigmoid(proj[..., o7:])
    qa = _partial_rope(_rmsnorm(qa, a_qnorm_g), pos)
    ka = _partial_rope(_rmsnorm(ka, a_knorm_g), pos)
    if past is None:
        ka_all, va_all, ks_all, vs_all = ka, va, ks, vs
    else:
        ka_all = jnp.concatenate([past[0].astype(ka.dtype), ka], axis=1)
        va_all = jnp.concatenate([past[1].astype(va.dtype), va], axis=1)
        ks_all = jnp.concatenate([past[2].astype(ks.dtype), ks], axis=1)
        vs_all = jnp.concatenate([past[3].astype(vs.dtype), vs], axis=1)
    lam = (jnp.exp(jnp.sum(a_lam_q1.astype(jnp.float32) * a_lam_k1.astype(jnp.float32)))
           - jnp.exp(jnp.sum(a_lam_q2.astype(jnp.float32) * a_lam_k2.astype(jnp.float32))) + lam_init)
    oa = _diff_attention(qa, ka_all, va_all, q_off, lam, lam_init, a_subln_g).astype(x.dtype)
    ob = _stick_breaking(qs, ks_all, vs_all, q_off).astype(x.dtype)
    mix = gate_a * (oa.reshape(bsz, t, A_VW) @ w_oa) + gate_b * (ob.reshape(bsz, t, B_W) @ w_ob)
    x = x + g1 * (mix @ w_out)
    h2 = _rmsnorm(x, norm2_g) * (1.0 + sc2) + sh2
    x = x + g2 * _hier_moe(h2, w_rg, b_rg, w_re, b_re, w1, w3, w2)
    return x, (ka, va, ks, vs)

def setup_inputs(seed: int = 0) -> dict:
    key = jax.random.key(seed)
    ks = jax.random.split(key, 32)
    f32 = jnp.float32

    def nrm(k, shape, scale):
        return jax.random.normal(k, shape, dtype=f32) * scale

    D = D_MODEL
    return {
        'x_prompt': nrm(ks[0], (BATCH, SEQ, D), 1.0),
        'x_sample': nrm(ks[1], (DEC_BATCH, DEC_SEQ, D), 1.0),
        'cache_a_k': nrm(ks[2], (DEPTH, DEC_BATCH, PAST_LEN, 2 * A_HEADS, A_DH), 1.0),
        'cache_a_v': nrm(ks[3], (DEPTH, DEC_BATCH, PAST_LEN, A_HEADS, A_DV), 1.0),
        'cache_b_k': nrm(ks[4], (DEPTH, DEC_BATCH, PAST_LEN, B_HEADS, B_DH), 1.0),
        'cache_b_v': nrm(ks[5], (DEPTH, DEC_BATCH, PAST_LEN, B_HEADS, B_DH), 1.0),
        'c_prompt': nrm(ks[6], (BATCH, D), 1.0),
        'c_sample': nrm(ks[7], (DEC_BATCH, D), 1.0),
        'norm1_g': 1.0 + nrm(ks[8], (DEPTH, D), 0.02),
        'norm2_g': 1.0 + nrm(ks[9], (DEPTH, D), 0.02),
        'w_ada': nrm(ks[10], (DEPTH, D, 6 * D), 0.5 * D ** -0.5),
        'b_ada': nrm(ks[11], (DEPTH, 6 * D), 0.02),
        'w_in': nrm(ks[12], (DEPTH, D, IN_COLS), D ** -0.5),
        'a_qnorm_g': 1.0 + nrm(ks[13], (DEPTH, A_DH), 0.02),
        'a_knorm_g': 1.0 + nrm(ks[14], (DEPTH, A_DH), 0.02),
        'a_lam_q1': nrm(ks[15], (DEPTH, A_DH), 0.1),
        'a_lam_k1': nrm(ks[16], (DEPTH, A_DH), 0.1),
        'a_lam_q2': nrm(ks[17], (DEPTH, A_DH), 0.1),
        'a_lam_k2': nrm(ks[18], (DEPTH, A_DH), 0.1),
        'a_subln_g': 1.0 + nrm(ks[19], (DEPTH, A_DV), 0.02),
        'w_oa': nrm(ks[20], (DEPTH, A_VW, D), A_VW ** -0.5),
        'w_ob': nrm(ks[21], (DEPTH, B_W, D), B_W ** -0.5),
        'w_out': nrm(ks[22], (DEPTH, D, D), D ** -0.5),
        'w_rg': nrm(ks[23], (DEPTH, D, N_GROUPS), D ** -0.5),
        'b_rg': nrm(ks[24], (DEPTH, N_GROUPS), 0.01),
        'w_re': nrm(ks[25], (DEPTH, D, N_EXPERTS), D ** -0.5),
        'b_re': nrm(ks[26], (DEPTH, N_EXPERTS), 0.01),
        'w1': nrm(ks[27], (DEPTH, N_EXPERTS, D, D_EXPERT), D ** -0.5),
        'w3': nrm(ks[28], (DEPTH, N_EXPERTS, D, D_EXPERT), D ** -0.5),
        'w2': nrm(ks[29], (DEPTH, N_EXPERTS, D_EXPERT, D), D_EXPERT ** -0.5),
    }

def reference(x_prompt, x_sample, cache_a_k, cache_a_v, cache_b_k, cache_b_v, c_prompt, c_sample,
              norm1_g, norm2_g, w_ada, b_ada, w_in, a_qnorm_g, a_knorm_g, a_lam_q1, a_lam_k1,
              a_lam_q2, a_lam_k2, a_subln_g, w_oa, w_ob, w_out, w_rg, b_rg, w_re, b_re, w1, w3, w2):
    xp = x_prompt
    xs = x_sample
    rows_p = ([], [], [], [])
    rows_s = ([], [], [], [])
    for l in range(DEPTH):
        lam_init = 0.8 - 0.6 * math.exp(-0.3 * l)
        params = (norm1_g[l], norm2_g[l], w_ada[l], b_ada[l], w_in[l], a_qnorm_g[l], a_knorm_g[l],
                  a_lam_q1[l], a_lam_k1[l], a_lam_q2[l], a_lam_k2[l], a_subln_g[l], w_oa[l], w_ob[l],
                  w_out[l], w_rg[l], b_rg[l], w_re[l], b_re[l], w1[l], w3[l], w2[l])
        xp, new_p = _layer(xp, c_prompt, None, lam_init, *params)
        past = (cache_a_k[l], cache_a_v[l], cache_b_k[l], cache_b_v[l])
        xs, new_s = _layer(xs, c_sample, past, lam_init, *params)
        for lst, r in zip(rows_p, new_p):
            lst.append(r)
        for lst, r in zip(rows_s, new_s):
            lst.append(r)
    return (xp, xs,
            jnp.stack(rows_p[0]), jnp.stack(rows_p[1]), jnp.stack(rows_p[2]), jnp.stack(rows_p[3]),
            jnp.stack(rows_s[0]), jnp.stack(rows_s[1]), jnp.stack(rows_s[2]), jnp.stack(rows_s[3]))


_drawn_inputs = setup_inputs


def setup_inputs(seed=0):
    import zlib

    import numpy as np

    out = dict(_drawn_inputs(seed))
    spreads = {}
    factors = {'cache_b_k': 7.11,
     'cache_b_v': 3.284,
     'norm1_g': 3.039,
     'norm2_g': 6.121,
     'a_qnorm_g': 8.0,
     'a_knorm_g': 2.926,
     'a_lam_q1': 7.977,
     'a_lam_k1': 8.0,
     'a_lam_q2': 8.0,
     'a_lam_k2': 8.0,
     'a_subln_g': 8.0,
     'b_rg': 8.0,
     'b_re': 8.0,
     'cache_a_k': 8.0,
     'cache_a_v': 8.0}
    for name, (base, spread) in spreads.items():
        noise = np.random.default_rng([zlib.crc32(name.encode()), seed]).standard_normal(out[name].shape)
        drawn = base * np.exp(spread * noise) if base else spread * noise
        out[name] = __import__('jax').numpy.asarray(drawn.astype(out[name].dtype))
    for name, factor in factors.items():
        out[name] = (out[name] * factor).astype(out[name].dtype)
    return out
```

```python
from contextlib import ExitStack

import numpy as np

import concourse.bass as bass
from concourse import mybir

P = 128
D = 1024
KD = D // P
SEQ, DEC, PAST = 256, 64, 256
TOK = SEQ + DEC
TILES = 3
PADDED = TILES * P
A_HEADS, B_PAIRS = 8, 8
GROUPS, PER_GROUP = 4, 8
EXPERTS = GROUPS * PER_GROUP
FE = 256
SLOTS = 64
MAX_ROUNDS = TOK // SLOTS
EPS = 1e-6
NEG = -1e30
LAM_INIT = 0.2
ADA_COLS = 256
UNIT = 3 * P
MIX_COLS = 256

ALU = mybir.AluOpType
ACT = mybir.ActivationFunctionType
AX = mybir.AxisListType.X
F32 = mybir.dt.float32
F32R = mybir.dt.float32r
I32 = mybir.dt.int32
U32 = mybir.dt.uint32

C_ID, C_TRI, C_LT, C_ROPEC, C_ROPES = 0, 128, 256, 384, 432
C_TOK, C_THR, C_W4, C_W8, C_E = 480, 483, 488, 492, 500
C_ALL = 532


def shape_constants():
    c = np.zeros((P, C_ALL), np.float32)
    r = np.arange(P)
    c[:, C_ID:C_ID + P] = np.eye(P)
    c[:, C_TRI:C_TRI + P] = -(r[:, None] >= r[None, :]).astype(np.float32)
    c[:, C_LT:C_LT + P] = (r[:, None] < r[None, :]).astype(np.float32)
    half = 8
    inv = np.exp(np.float32(-np.log(500000.0) * 2.0) * np.arange(half, dtype=np.float32) / np.float32(16))
    pos = (np.arange(TILES)[None, :] * P + r[:, None]).astype(np.float32)
    ang = (pos[:, :, None] * inv.astype(np.float32)).astype(np.float32)
    cos, sin = np.cos(ang), np.sin(ang)
    c[:, C_ROPEC:C_ROPEC + 48] = np.concatenate([cos, cos], 2).reshape(P, 48)
    c[:, C_ROPES:C_ROPES + 48] = np.concatenate([-sin, sin], 2).reshape(P, 48)
    c[:, C_TOK:C_TOK + 3] = pos
    c[:, C_THR:C_THR + MAX_ROUNDS] = np.arange(MAX_ROUNDS) * SLOTS
    c[:, C_W4:C_W4 + 4] = 4 - np.arange(4)
    c[:, C_W8:C_W8 + 8] = 8 - np.arange(8)
    c[:, C_E:C_E + 32] = np.arange(32)
    return c


def rows_of(t):
    return P if t < 2 else DEC


def build(nc, t_in, t_out):
    g = t_in
    ctx = ExitStack()
    with ctx:
        def sem(name):
            return ctx.enter_context(nc.semaphore(name))

        top = nc.sbuf_base
        end = top + nc.sbuf_bytes_remaining

        def place(name, shape, dt, at):
            assert at + 4 * int(np.prod(shape[1:])) <= end, name
            return nc.alloc_sbuf_tensor_at(name, shape, dt, offset=at)

        cursor = [(top + 31) // 32 * 32]

        def take(name, shape, dt=F32):
            at = cursor[0]
            cursor[0] += (4 * int(np.prod(shape[1:])) + 31) // 32 * 32
            return place(name, shape, dt, at)

        cst = take("cst", [P, C_ALL])
        ident = cst[:, C_ID:C_ID + P]
        tri_neg = cst[:, C_TRI:C_TRI + P]
        before = cst[:, C_LT:C_LT + P]
        ones = take("ones", [P, P])
        ones_neg = take("ones_neg", [P, P])
        eps = take("eps", [P, 1])
        lam_rows = take("lam_rows", [P, 4, 64])
        lam_prod = take("lam_prod", [P, 2, 64])
        lam_sum = take("lam_sum", [P, 2])
        lam_exp = take("lam_exp", [P, 2])
        neg_lam = take("neg_lam", [P, 1])
        gqk = take("gqk", [P, 4, 64])
        vec_rows = take("vec_rows", [80, P])
        vec_cols = take("vec_cols", [P, 80])
        subln = take("subln", [P, 1])
        c_sig = take("c_sig", [80, P])
        mod = take("mod", [P, 48, 2])
        gain1 = take("gain1", [P, KD, 2])
        gain2 = take("gain2", [P, KD, 2])
        stat = take("stat", [P, 3])
        stat_ln = take("stat_ln", [P, 3])
        rstd = take("rstd", [P, 3])
        rw = take("rw", [P, KD, 36])
        rb = take("rb", [1, 36])
        zero = take("zero", [P, 3 * MAX_ROUNDS * SLOTS * EXPERTS // P])

        x_sb = take("x_sb", [P, TILES, D])
        xnT = take("xnT", [P, KD, PADDED])
        hT_hi = take("hT_hi", [P, KD, PADDED], F32R)
        hT_lo = take("hT_lo", [P, KD, PADDED], F32R)
        oT_hi = take("oT_hi", [P, KD, TOK], F32R)
        oT_lo = take("oT_lo", [P, KD, TOK], F32R)
        hT_at = cursor[0] - 4 * (2 * KD * PADDED + 2 * KD * TOK)
        raw_at = cursor[0]
        raw = [take(f"raw{j}", [P, KD, UNIT]) for j in range(2)]
        split_at = cursor[0]
        w_hi = [take(f"w_hi{j}", [P, KD, UNIT], F32R) for j in range(2)]
        w_lo = [take(f"w_lo{j}", [P, KD, UNIT], F32R) for j in range(2)]
        attn_at = cursor[0]

        stage = [take(f"stage{j}", [P, TILES, UNIT]) for j in range(2)]
        a_kc = [take(f"a_kc{j}", [P, 2, P]) for j in range(2)]
        a_vc = [take(f"a_vc{j}", [P, 2, P]) for j in range(2)]
        qkT = take("qkT", [P, 1024])
        sq = take("sq", [P, TILES, 256])
        ss = take("ss", [P, 12])
        ss_ln = take("ss_ln", [P, 12])
        rs = take("rs", [P, 12])
        rope_x = take("rope_x", [P, TILES, 4, 16])
        rope_y = take("rope_y", [P, TILES, 4, 16])
        probs = [take(f"probs{m}", [P, 704]) for m in range(2)]
        amap = take("amap", [P, 768])
        aT = take("aT", [P, 768])
        v_keep = [take(f"v_keep{j}", [P, TILES, P]) for j in range(2)]
        a_mx = take("a_mx", [P, 2, 3])
        a_nmx = take("a_nmx", [P, 2, 3])
        a_sum = take("a_sum", [P, 2, 3])
        a_rec = take("a_rec", [P, 2, 3])
        osq = take("osq", [P, TILES, P])
        o_ss = take("o_ss", [P, 3])
        o_ln = take("o_ln", [P, 3])
        o_rs = take("o_rs", [P, 3])
        o_n = take("o_n", [P, TILES, P])
        a_end = cursor[0]

        ada_buf = [place(f"ada_buf{n}", [P, KD, ADA_COLS], F32, hT_at + 4 * KD * ADA_COLS * n) for n in range(4)]
        assert hT_at + 16 * KD * ADA_COLS <= raw_at
        ada_late = [take(f"ada_late{n}", [P, KD, ADA_COLS]) for n in range(2)]
        cursor[0] = a_end

        xn = place("xn", [P, TILES, D], F32, attn_at)

        cursor[0] = attn_at
        b_qT = [take(f"b_qT{j}", [P, TOK]) for j in range(2)]
        b_kT = [take(f"b_kT{j}", [P, 640]) for j in range(2)]
        b_v = [take(f"b_v{j}", [P, TILES, P]) for j in range(2)]
        b_ktok = [take(f"b_ktok{j}", [P, TILES, P]) for j in range(2)]
        b_kc = [take(f"b_kc{j}", [P, 2, P]) for j in range(2)]
        b_vc = [take(f"b_vc{j}", [P, 2, P]) for j in range(2)]
        z_na = [take(f"z_na{f}", [P, 2, n]) for f, n in ((0, 384), (1, 192))]
        z_sp = [take(f"z_sp{f}", [P, 2, n]) for f, n in ((0, 384), (1, 192))]
        z_w = [take(f"z_w{f}", [P, 2, n]) for f, n in ((0, 384), (1, 192))]
        b_end = cursor[0]

        sig = [place(f"sig{m}", [P, TOK], F32, attn_at + 4 * TOK * m) for m in range(2)]
        sig_r = [place(f"sig_r{m}", [P, TOK], F32, attn_at + 4 * TOK * (2 + m)) for m in range(2)]
        late = attn_at + 16 * TOK
        g1b = place("g1b", [P, 2, D], F32, late)
        wtmp = place("wtmp", [P, TILES, MIX_COLS], F32, late + 8192)
        cursor[0] = raw_at
        ew = []
        for q in range(4):
            ew.append((take(f"e{q}_w1", [P, KD, FE]), take(f"e{q}_w3", [P, KD, FE]), take(f"e{q}_w2", [P, 2, D])))
        cursor[0] = max(cursor[0], late + 8192 + 4 * TILES * MIX_COLS)
        moe_at = cursor[0]
        g2b = take("g2b", [P, 2, D])
        cursor[0] = hT_at
        h2tok = take("h2tok", [P, TILES, D])
        xn2 = place("xn2", [P, TILES, D], F32, cursor[0])
        ya = take("ya", [P, TILES, D])
        yb = h2tok
        xg = [take(f"xg{q}", [SLOTS, D]) for q in range(4)]
        xgT = [take(f"xgT{j}", [P, KD, SLOTS]) for j in range(2)]
        assert cursor[0] <= raw_at
        cursor[0] = moe_at + 8192
        y_sb = [take(f"y_sb{j}", [SLOTS, D]) for j in range(2)]
        hid = [take(f"hid{j}", [P, 2, SLOTS]) for j in range(2)]
        h_e = [take(f"h_e{j}", [P, 2 * SLOTS]) for j in range(2)]
        h_s = [take(f"h_s{j}", [P, 2 * SLOTS]) for j in range(2)]
        lg = take("lg", [P, TILES, 36])
        gmax = take("gmax", [P, TILES])
        lsub = take("lsub", [P, TILES, 4])
        pgsum = take("pgsum", [P, TILES])
        pg = take("pg", [P, TILES])
        g1h = take("g1h", [P, TILES, 4])
        gtie = take("gtie", [P, TILES, 4])
        gtm = take("gtm", [P, TILES])
        lsel4 = take("lsel4", [P, TILES, 4, 8])
        lsel = take("lsel", [P, TILES, 8])
        etie = take("etie", [P, TILES, 8])
        etm = take("etm", [P, TILES])
        m1 = take("m1", [P, TILES])
        m2 = take("m2", [P, TILES])
        eh1 = take("eh1", [P, TILES, 8])
        eh2 = take("eh2", [P, TILES, 8])
        e2 = take("e2", [P, TILES])
        wsum = take("wsum", [P, TILES])
        pair = [take(f"pair{j}", [P, TILES, 3]) for j in range(2)]
        E1 = [take(f"E{j}", [P, TILES, EXPERTS]) for j in range(2)]
        M = take("M", [P, TILES, EXPERTS])
        rank = take("rank", [P, TILES, EXPERTS])
        rtmp = take("rtmp", [P, TILES, EXPERTS])
        posf = take("posf", [P, 2, TILES])
        posi = take("posi", [P, 2, TILES], U32)
        cnt = take("cnt", [P, 1])
        thr = take("thr", [P, MAX_ROUNDS])
        rnd = take("rnd", [P, 1])
        rnd_i = take("rnd_i", [P, 1], I32)
        tab = take("tab", [SLOTS, EXPERTS, 3])
        tab_i = take("tab_i", [SLOTS, EXPERTS, 2], U32)
        idx = [take(f"idx{q}", [SLOTS, 1], U32) for q in range(4)]
        row_idx = [take(f"row_idx{j}", [SLOTS, 1], U32) for j in range(2)]
        assert cursor[0] <= end, (cursor[0], end)

        ps = ctx.enter_context(nc.psum_tensor("ps", [P, 8, 512], F32))
        h2_dram = nc.dram_tensor("h2_rows", [PADDED, D], F32).ap()
        tab_dram = nc.dram_tensor("slot_table", [MAX_ROUNDS * SLOTS * EXPERTS, 3], F32).ap()
        y_dram = nc.dram_tensor("expert_rows", [1 + 2 * TOK, D], F32).ap()

        small_in = sem("small_in"); rows_in = sem("rows_in"); x_in = sem("x_in"); router_in = sem("router_in")
        setup_done = sem("setup_done"); zero_ready = sem("zero_ready")
        c_act = sem("c_act"); c_dve = sem("c_dve"); vecT_done = sem("vecT_done"); vec_ready = sem("vec_ready")
        raw_loaded = [sem(f"raw_loaded{j}") for j in range(2)]
        ada_in = [sem(f"ada_in{n}") for n in range(4)]; late_in = [sem(f"late_in{n}") for n in range(2)]
        ada_used = sem("ada_used"); late_used = sem("late_used"); mod_ready = sem("mod_ready")
        lam_dve = sem("lam_dve"); lam_act = sem("lam_act")
        n_rstd = sem("n_rstd"); n_scaled = sem("n_scaled"); n_T = sem("n_T")
        n_out_a = sem("n_out_a"); n_out_v = sem("n_out_v")
        h_full = sem("h_full"); h_hi = sem("h_hi"); h_ready = sem("h_ready")
        split_hi = sem("split_hi"); split_done = sem("split_done"); unit_used = sem("unit_used")
        a_cache = [sem(f"a_cache{j}") for j in range(2)]
        a_proj = sem("a_proj"); a_staged = sem("a_staged")
        a_sq = sem("a_sq"); a_ss = sem("a_ss"); a_rs = sem("a_rs"); a_scaled = sem("a_scaled"); a_roped = sem("a_roped")
        a_stored = [sem(f"a_stored{j}") for j in range(2)]
        a_qkT = sem("a_qkT"); a_qkT_act = sem("a_qkT_act"); a_qkT_dve = sem("a_qkT_dve")
        a_s = [sem(f"a_s{f}") for f in range(2)]
        a_max = [sem(f"a_max{f}") for f in range(2)]
        a_exp = [sem(f"a_exp{f}") for f in range(2)]
        a_comb = sem("a_comb")
        a_aT = sem("a_aT"); a_aT_act = sem("a_aT_act"); a_aT_dve = sem("a_aT_dve")
        a_vkept = sem("a_vkept"); a_pv = sem("a_pv"); a_osq = sem("a_osq"); a_oss = sem("a_oss"); a_ors = sem("a_ors"); a_on = sem("a_on")
        a_oT = sem("a_oT"); a_ohi = sem("a_ohi"); a_olo = sem("a_olo")
        b_cache = [sem(f"b_cache{j}") for j in range(2)]
        b_q = sem("b_q"); b_k = sem("b_k"); b_vp = sem("b_vp")
        b_q_out = sem("b_q_out"); b_k_out = sem("b_k_out"); b_v_out = sem("b_v_out")
        b_tk = sem("b_tk"); b_tk_out = sem("b_tk_out"); b_tc = sem("b_tc"); b_tc_out = sem("b_tc_out")
        b_stored = [sem(f"b_stored{j}") for j in range(2)]
        b_z = sem("b_z"); b_zero = sem("b_zero"); b_l = sem("b_l"); b_sp = sem("b_sp"); b_spm = sem("b_spm")
        b_c = sem("b_c"); b_w = sem("b_w"); b_wm = sem("b_wm"); b_o = sem("b_o"); b_ohi = sem("b_ohi"); b_olo = sem("b_olo")
        x_g = sem("x_g"); x_o = sem("x_o"); x_e = sem("x_e"); x_mix = sem("x_mix")
        m_hi = sem("m_hi"); m_ready = sem("m_ready")
        gb_done = sem("gb_done"); gb_ready = sem("gb_ready")
        o_done = sem("o_done"); o_added = sem("o_added")
        h2_ready = sem("h2_ready"); r_T = sem("r_T"); r_rows = sem("r_rows"); 
        r_log = sem("r_log"); r_sub = sem("r_sub"); r_exp = sem("r_exp"); r_e2 = sem("r_e2"); r_e2x = sem("r_e2x")
        r_M = sem("r_M"); r_rank = sem("r_rank"); r_pos = sem("r_pos"); rounds_ready = sem("rounds_ready")
        tab_zero = sem("tab_zero"); tab_put = sem("tab_put"); tab_in = sem("tab_in"); tab_ready = sem("tab_ready")
        idx_ready = [sem(f"idx_ready{j}") for j in range(2)]; row_ready = [sem(f"row_ready{j}") for j in range(2)]
        ew_loaded = [sem(f"ew_loaded{q}") for q in range(4)]
        ew_used = [sem(f"ew_used{q}") for q in range(4)]
        gathered = [sem(f"gathered{q}") for q in range(4)]
        e_T = [sem(f"e_T{j}") for j in range(2)]
        e_xT = [sem(f"e_xT{j}") for j in range(2)]
        e_h = [sem(f"e_h{j}") for j in range(2)]
        e_exp = [sem(f"e_exp{j}") for j in range(2)]
        e_hid = [sem(f"e_hid{j}") for j in range(2)]
        e_y = [sem(f"e_y{j}") for j in range(2)]
        e_out_a = [sem(f"e_out_a{j}") for j in range(2)]
        e_out_v = [sem(f"e_out_v{j}") for j in range(2)]
        y_stored = [sem(f"y_stored{j}") for j in range(2)]
        back = sem("back"); y_done = sem("y_done"); stored = sem("stored")

        S_A, S_MIXA, S_B, S_MIXB, S_OUT = 0, 8, 16, 24, 32

        w_in3 = g["w_in"].rearrange("(k p) n -> p k n", p=P)
        w_ada3 = g["w_ada"].rearrange("(k p) n -> p k n", p=P)
        prj3 = [g[n].rearrange("(k p) n -> p k n", p=P) for n in ("w_oa", "w_ob", "w_out")]

        def f32(ap):
            return ap.bitcast(F32)

        block = ctx.enter_context(nc.Block())

        @block.sync
        def _(sp):
            sp.dma_start(cst[:], g["shape_constants"]).then_inc(small_in, 16)
            sp.dma_start(vec_rows[64:72, :], g["c_prompt"].rearrange("a (k p) -> (a k) p", p=P)).then_inc(small_in, 16)
            sp.dma_start(vec_rows[72:80, :], g["c_sample"].rearrange("a (k p) -> (a k) p", p=P)).then_inc(small_in, 16)
            sp.dma_start(vec_rows[0:48, :], g["b_ada"].rearrange("(k p) -> k p", p=P)).then_inc(small_in, 16)
            sp.dma_start(vec_rows[48:56, :], g["norm1_g"].rearrange("(k p) -> k p", p=P)).then_inc(small_in, 16)
            sp.dma_start(vec_rows[56:64, :], g["norm2_g"].rearrange("(k p) -> k p", p=P)).then_inc(small_in, 16)

            def load_unit(base, h, j):
                for n in range(3):
                    sp.dma_start(raw[j][:, :, n * P:(n + 1) * P],
                                 w_in3[:, :, bass.ds(base + n * D + h * P, P)]).then_inc(raw_loaded[j], 16)

            def load_ada(c):
                sp.dma_start(ada_buf[c % 4][:], w_ada3[:, :, c * ADA_COLS:(c + 1) * ADA_COLS]).then_inc(ada_in[c % 4], 16)

            def load_late(h, n):
                if not (isinstance(h, int) and h == 0):
                    sp.wait_ge(late_used, 2 * h + n - 1)
                sp.dma_start(ada_late[n][:], w_ada3[:, :, bass.ds((8 + 2 * h + n) * ADA_COLS, ADA_COLS)]).then_inc(late_in[n], 16)

            load_ada(0)
            load_ada(1)
            sp.dma_start(x_sb[:, 0:2, :], g["x_prompt"][0].rearrange("(t p) d -> p t d", p=P)).then_inc(x_in, 16)
            sp.dma_start(x_sb[0:DEC, 2, :], g["x_sample"][0]).then_inc(x_in, 16)
            for n, name in enumerate(("a_lam_q1", "a_lam_k1", "a_lam_q2", "a_lam_k2")):
                sp.dma_start(lam_rows[:, n, :], g[name].partition_broadcast(P)).then_inc(rows_in, 16)
            for n in range(4):
                sp.dma_start(gqk[:, n, :], g["a_qnorm_g" if n < 2 else "a_knorm_g"].partition_broadcast(P)).then_inc(rows_in, 16)
            sp.dma_start(subln[:], g["a_subln_g"].rearrange("(p a) -> p a", a=1)).then_inc(rows_in, 16)
            sp.dma_start(rw[:, :, 0:4], g["w_rg"].rearrange("(k p) n -> p k n", p=P)).then_inc(router_in, 16)
            sp.dma_start(rw[:, :, 4:36], g["w_re"].rearrange("(k p) n -> p k n", p=P)).then_inc(router_in, 16)
            sp.dma_start(rb[:, 0:4], g["b_rg"].rearrange("(a n) -> a n", a=1)).then_inc(router_in, 16)
            sp.dma_start(rb[:, 4:36], g["b_re"].rearrange("(a n) -> a n", a=1)).then_inc(router_in, 16)
            sp.wait_ge(zero_ready, 1)
            sp.dma_start(tab_dram.rearrange("(p n) a -> p (n a)", p=P), zero[:]).then_inc(tab_zero, 16)
            load_ada(2)
            load_ada(3)
            load_unit(0, 0, 0)
            for c in range(4, 8):
                sp.wait_ge(ada_used, c - 3)
                load_ada(c)
            load_unit(0, 1, 1)

            def load_prj(j, src, c):
                sp.dma_start(raw[j][:, :, 0:MIX_COLS], src[:, :, bass.ds(c * MIX_COLS, MIX_COLS)]).then_inc(raw_loaded[j], 48)

            def cache(kc, vc, ks, vs, h, s):
                sp.dma_start(kc[:], ks.rearrange("(t p) n -> p t n", p=P)[:, :, bass.ds(h * P, P)]).then_inc(s, 16)
                sp.dma_start(vc[:], vs.rearrange("(t p) n -> p t n", p=P)[:, :, bass.ds(h * P, P)]).then_inc(s, 16)

            def store(src_k, src_v, outs, h, s):
                kp, vp, kss, vss = outs
                for dst, src in ((kp, src_k), (vp, src_v)):
                    sp.dma_start(dst.rearrange("(t p) n -> p t n", p=P)[:, :, bass.ds(h * P, P)], src[:, 0:2, :]).then_inc(s, 16)
                for dst, src in ((kss, src_k), (vss, src_v)):
                    sp.dma_start(dst[:, bass.ds(h * P, P)], src[0:DEC, 2, :]).then_inc(s, 16)

            def a_cache_load(h, j, first):
                if not first:
                    sp.wait_ge(a_qkT, h - 1)
                    sp.wait_ge(a_pv, h - 1)
                cache(a_kc[j], a_vc[j], g["cache_a_k"], g["cache_a_v"], h, a_cache[j])

            def a_weights(h, j):
                sp.wait_ge(split_done, S_A + h + 1)
                load_unit(0, h + 2, j)

            def a_store(h, j):
                sp.wait_ge(a_roped, h + 1)
                store(stage[j][:, :, P:2 * P], stage[j][:, :, 2 * P:3 * P],
                      [t_out[n] for n in ("a_k_prompt", "a_v_prompt", "a_k_sample", "a_v_sample")], h, a_stored[j])

            sp.wait_ge(n_T, KD)
            a_cache_load(0, 0, True)
            a_cache_load(1, 1, True)
            a_weights(0, 0)
            a_weights(1, 1)
            a_store(0, 0)
            for n in range(2):
                load_late(0, n)
            with sp.Fori(1, 3) as i:
                for j in range(2):
                    a_weights(2 * i + j, j)
                    a_store(2 * i + j - 1, 1 - j)
                    a_cache_load(2 * i + j, j, False)
                    for n in range(2):
                        load_late(2 * i + j - 1, n)
            for j in range(2):
                sp.wait_ge(split_done, S_A + 7 + j)
                load_prj(j, prj3[0] if j else w_in3[:, :, 6 * D:7 * D], 0)
                a_store(5 + j, 1 - j)
                a_cache_load(6 + j, j, False)
                for n in range(2):
                    load_late(5 + j, n)
            a_store(7, 1)
            for n in range(2):
                load_late(7, n)

            def mix_loads(gate_col, prj, s0, c):
                for j in range(2):
                    units = sp.to_reg(s0 + 2 * c - 1 + j)
                    sp.wait_ge(small_in, 16)
                    sp.wait_ge(split_done, units)
                    load_prj(j, prj if j else w_in3[:, :, gate_col:gate_col + D], c)

            with sp.Fori(1, 4) as c:
                mix_loads(6 * D, prj3[0], S_MIXA, c)
            for j in range(2):
                sp.wait_ge(split_done, S_B - 1 + j)
                load_unit(3 * D, j, j)

            def b_iteration(p, j, load, first):
                if load:
                    sp.wait_ge(split_done, S_B + p + 1)
                    load_unit(3 * D, p + 2, j)
                if first:
                    sp.wait_ge(a_olo, A_HEADS)
                    sp.wait_ge(x_mix, 8)
                    sp.wait_ge(a_stored[j], 4 * 64)
                    sp.wait_ge(a_stored[1 - j], 4 * 64)
                else:
                    sp.wait_ge(b_tc, p - 1)
                    sp.wait_ge(b_o, p - 1)
                cache(b_kc[j], b_vc[j], g["cache_b_k"], g["cache_b_v"], p, b_cache[j])

            def b_store(p, j):
                sp.wait_ge(b_tk_out, p + 1)
                sp.wait_ge(b_v_out, p + 1)
                store(b_ktok[j][:], b_v[j][:],
                      [t_out[n] for n in ("b_k_prompt", "b_v_prompt", "b_k_sample", "b_v_sample")], p, b_stored[j])

            b_iteration(0, 0, True, True)
            b_iteration(1, 1, True, True)
            b_store(0, 0)
            with sp.Fori(1, 3) as i:
                for j in range(2):
                    b_iteration(2 * i + j, j, True, False)
                    b_store(2 * i + j - 1, 1 - j)
            for j in range(2):
                b_iteration(6 + j, j, False, False)
                sp.wait_ge(split_done, S_B + 7 + j)
                load_prj(j, prj3[1] if j else w_in3[:, :, 7 * D:8 * D], 0)
                b_store(5 + j, 1 - j)
            b_store(7, 1)
            with sp.Fori(1, 4) as c:
                mix_loads(7 * D, prj3[1], S_MIXB, c)
            for u in range(4):
                sp.wait_ge(split_done, S_OUT - 1 + u)
                load_prj(u % 2, prj3[2], u)

            def load_expert(q, e):
                w1s, w3s, w2s = ew[q]
                sp.dma_start(w1s[:], g["w1"].rearrange("e (p k) f -> e p k f", k=KD)[e]).then_inc(ew_loaded[q], 16)
                sp.dma_start(w3s[:], g["w3"].rearrange("e (p k) f -> e p k f", k=KD)[e]).then_inc(ew_loaded[q], 16)
                sp.dma_start(w2s[:], g["w2"].rearrange("e (p m) d -> e p m d", m=2)[e]).then_inc(ew_loaded[q], 16)

            sp.wait_ge(split_done, S_OUT + 4)
            sp.wait_ge(unit_used, S_OUT + 4)
            sp.wait_ge(o_added, 12)
            count = sp.alloc_register("sp_rounds")
            sp.reg_mov(count, 1)
            with sp.Fori(0, count) as r:
                with sp.Fori(0, 8) as i:
                    for q in range(4):
                        sp.wait_ge(ew_used[q], 8 * r + i + 1)
                        load_expert(q, 4 * i + q)
                sp.wait_ge(rounds_ready, 1)
                sp.reg_load(count, rnd_i[0:1, 0:1])
            sp.wait_ge(y_done, 2)
            sp.dma_start(t_out["y_prompt"].rearrange("(t p) d -> p t d", p=P), x_sb[:, 0:2, :]).then_inc(stored, 16)
            sp.dma_start(t_out["y_sample"], x_sb[0:DEC, 2, :]).then_inc(stored, 16)
            sp.wait_ge(stored, 32)
            for s in a_stored + b_stored:
                sp.wait_ge(s, 4 * 64)

        @block.tensor
        def _(pe):
            def bank(b):
                return ps[:, b, :]

            def mm3(out, lhs_hi, lhs_lo, rhs_hi, rhs_lo, first, last):
                nc.tensor.matmul(out, lhs_hi, rhs_hi, start=first, stop=False, skip_group_check=True)
                nc.tensor.matmul(out, lhs_hi, rhs_lo, start=False, stop=False, skip_group_check=True)
                return nc.tensor.matmul(out, lhs_lo, rhs_hi, start=False, stop=last, skip_group_check=True)

            def mm(out, lhs, rhs, first, last=True):
                return nc.tensor.matmul(out, lhs, rhs, start=first, stop=last, skip_group_check=True)

            for s in e_T + e_h + e_y + ew_used:
                pe.nop().then_inc(s, 1)
            pe.wait_ge(c_dve, 1)
            nc.tensor.transpose(ps[:, 0, 0:80], vec_rows[:], ident[0:80, 0:80]).then_inc(vecT_done, 1)
            pe.wait_ge(vec_ready, 1)

            def ada(buf, column, done):
                for m in range(2):
                    for k in range(KD):
                        last = mm(ps[:, 7, bass.ds(column + 2 * m, 2)], buf[:, k, m * P:(m + 1) * P],
                                  vec_cols[:, 64 + k:80:KD], k == 0, k == KD - 1)
                last.then_inc(done, 1)

            def rows_to_columns(src, k, b):
                for t in range(TILES):
                    last = nc.tensor.transpose(ps[:, b, t * P:(t + 1) * P], src[:, t, k * P:(k + 1) * P], ident)
                return last

            def first_chunks(i):
                for j in range(4):
                    pe.wait_ge(ada_in[j], 16 * (i + 1))
                    ada(ada_buf[j], 16 * i + 4 * j, ada_used)

            first_chunks(0)
            pe.wait_ge(n_scaled, 3)
            for k in range(KD - 1):
                rows_to_columns(xn, k, k).then_inc(n_T, 1)
            pe.wait_ge(n_out_a, 1)
            rows_to_columns(xn, KD - 1, 0).then_inc(n_T, 1)
            first_chunks(1)

            def ada_chunk(h, n):
                pe.wait_ge(late_in[n], 16 * (h - 2))
                ada(ada_late[n], 384 + 8 * (h - 3) + 4 * n, late_used)

            pe.wait_ge(h_ready, 2)

            def proj_tile(h, j, t, first):
                if t == 0:
                    pe.wait_ge(split_done, S_A + h + 1)
                if not first:
                    pe.wait_ge(a_staged, 3 * h - 2 + t)
                for k in range(KD):
                    sl = slice(t * P, (t + 1) * P)
                    last = mm3(ps[:, t, 0:UNIT], hT_hi[:, k, sl], hT_lo[:, k, sl], w_hi[j][:, k, :], w_lo[j][:, k, :],
                               k == 0, k == KD - 1)
                last.then_inc(a_proj, 1)
                if t == 2:
                    pe.drain()
                    pe.nop().then_inc(unit_used, 1)

            def a_iteration(h, j, P_on, qk_on, s1_on, o_on, cache_value):
                jq = 1 - j
                if P_on:
                    proj_tile(h, j, 0, isinstance(h, int) and h == 0)
                if o_on:
                    l = h - 3
                    pe.wait_ge(a_aT_act, l + 1)
                    pe.wait_ge(a_aT_dve, l + 1)
                    pe.wait_ge(a_vkept, l + 1)
                    pe.wait_ge(a_on, l)
                    v, vc = v_keep[jq], a_vc[jq]
                    for t, pairs in ((0, ((0, v[:, 0, :]),)), (1, ((1, v[:, 0, :]), (2, v[:, 1, :]))),
                                     (2, ((3, vc[:, 0, :]), (4, vc[:, 1, :]), (5, v[:, 2, :])))):
                        for n, (blk, rhs) in enumerate(pairs):
                            last = mm(ps[:, 7, t * P:(t + 1) * P], aT[:, blk * P:(blk + 1) * P], rhs,
                                      n == 0, n == len(pairs) - 1)
                    last.then_inc(a_pv, 1)
                if s1_on:
                    pe.wait_ge(a_exp[0], h - 1)
                    for mp in range(2):
                        r = slice(64 * mp, 64 * mp + 64)
                        last = mm(ps[:, 5 + mp, 0:320], qkT[r, 256:384], qkT[r, 640:960], True)
                    last.then_inc(a_s[1], 1)
                if P_on:
                    proj_tile(h, j, 1, isinstance(h, int) and h == 0)
                if o_on:
                    l = h - 3
                    pe.wait_ge(a_on, l + 1)
                    for t in range(TILES):
                        last = nc.tensor.transpose(ps[:, 4, t * P:(t + 1) * P], o_n[:, t, :], ident)
                    last.then_inc(a_oT, 1)
                    ada_chunk(h, 0)
                if qk_on:
                    m = h - 1
                    pe.wait_ge(a_roped, m + 1)
                    pe.wait_ge(a_cache[jq], cache_value)
                    st = stage[jq]
                    for n, src in enumerate((st[:, 0, 0:P], st[:, 1, 0:P], st[:, 2, 0:P], st[:, 0, P:2 * P])):
                        nc.tensor.transpose(ps[:, 3, n * P:(n + 1) * P], src, ident)
                    if o_on:
                        ada_chunk(h, 1)
                        pe.wait_ge(a_olo, h - 2)
                    for n, src in enumerate((st[:, 1, P:2 * P], a_kc[jq][:, 0, :], a_kc[jq][:, 1, :], st[:, 2, P:2 * P])):
                        last = nc.tensor.transpose(ps[:, 4, n * P:(n + 1) * P], src, ident)
                    last.then_inc(a_qkT, 1)
                elif o_on:
                    ada_chunk(h, 1)
                if P_on:
                    proj_tile(h, j, 2, isinstance(h, int) and h == 0)
                if s1_on:
                    pe.wait_ge(a_comb, 2 * h - 2)
                    if qk_on:
                        pe.wait_ge(a_qkT_act, h)
                        pe.wait_ge(a_qkT_dve, h)
                    elif o_on:
                        pe.wait_ge(a_olo, h - 2)
                    for n in range(6):
                        b, c = (3, n) if n < 4 else (4, n - 4)
                        last = nc.tensor.transpose(ps[:, b, c * P:(c + 1) * P], amap[:, n * P:(n + 1) * P], ident)
                    last.then_inc(a_aT, 1)
                if qk_on:
                    pe.wait_ge(a_qkT_act, h)
                    pe.wait_ge(a_qkT_dve, h)
                    if s1_on:
                        pe.wait_ge(a_exp[1], h - 1)
                    for mp in range(2):
                        r = slice(64 * mp, 64 * mp + 64)
                        mm(ps[:, 5 + mp, 0:128], qkT[r, 0:128], qkT[r, 384:512], True)
                        last = mm(ps[:, 5 + mp, 128:384], qkT[r, 128:256], qkT[r, 384:640], False)
                    last.then_inc(a_s[0], 1)

            for h in range(4):
                a_iteration(h, h % 2, True, h >= 1, h >= 2, h >= 3, 32 * ((h - 1) // 2 + 1))
            with pe.Fori(2, 4) as i:
                for j in range(2):
                    a_iteration(2 * i + j, j, True, True, True, True, 32 * (i + j))
            for h in range(8, 11):
                a_iteration(h, h % 2, False, h < 9, h < 10, True, 128)

            def mix(c, s0, first):
                for j, (rhs_hi, rhs_lo, done) in enumerate(((hT_hi, hT_lo, x_g), (oT_hi, oT_lo, x_o))):
                    pe.wait_ge(split_done, s0 + 2 * c + j + 1)
                    if not first:
                        pe.wait_ge(x_e if j == 0 else x_mix, first_mix[0] + 2 * c)
                    for m in range(2):
                        sl = slice(m * P, (m + 1) * P)
                        for k in range(KD):
                            last = mm3(ps[:, 2 * j + m, 0:TOK], w_hi[j][:, k, sl], w_lo[j][:, k, sl],
                                       rhs_hi[:, k, 0:TOK], rhs_lo[:, k, 0:TOK], k == 0, k == KD - 1)
                    last.then_inc(done, 1)
                    pe.drain()
                    pe.nop().then_inc(unit_used, 1)

            first_mix = [0]
            pe.wait_ge(a_staged, 24)
            pe.wait_ge(a_olo, 8)
            mix(0, S_MIXA, True)
            with pe.Fori(1, 4) as c:
                mix(c, S_MIXA, False)

            def b_iteration(p, j, P_on, z_on, w_on, first, cache_value):
                jz = 1 - j
                if P_on:
                    pe.wait_ge(split_done, S_B + p + 1)
                    if first:
                        pe.wait_ge(x_e, 8)
                        pe.wait_ge(x_mix, 8)
                    else:
                        pe.wait_ge(b_v_out, p)
                    for k in range(KD):
                        last = mm3(ps[:, 0, 0:TOK], w_hi[j][:, k, 0:P], w_lo[j][:, k, 0:P],
                                   hT_hi[:, k, 0:TOK], hT_lo[:, k, 0:TOK], k == 0, k == KD - 1)
                    last.then_inc(b_q, 1)
                if w_on:
                    l = p - 2
                    pe.wait_ge(b_wm, l + 1)
                    if not (isinstance(p, int) and p == 2):
                        pe.wait_ge(b_olo, l)
                    v, vc = b_v[j], b_vc[j]
                    for hh in range(2):
                        c = slice(64 * hh, 64 * hh + 64)
                        o = ps[c, 3, :]
                        mm(o[:, 0:256], v[:, 0, c], z_w[0][:, hh, 0:256], True)
                        mm(o[:, 128:256], v[:, 1, c], z_w[0][:, hh, 256:384], False)
                        mm(o[:, 256:320], vc[:, 0, c], z_w[1][:, hh, 0:64], False)
                        mm(o[:, 256:320], vc[:, 1, c], z_w[1][:, hh, 64:128], False)
                        last = mm(o[:, 256:320], v[:, 2, c], z_w[1][:, hh, 128:192], False)
                    last.then_inc(b_o, 1)
                if z_on:
                    pe.wait_ge(b_q_out, p)
                    pe.wait_ge(b_k_out, p)
                    pe.wait_ge(b_tc_out, p)
                    if isinstance(p, int) and p == 1:
                        pe.wait_ge(b_zero, 1)
                    if w_on:
                        pe.wait_ge(b_w, p - 1)
                    kT, qT = b_kT[jz], b_qT[jz]
                    for hh in range(2):
                        r = slice(64 * hh, 64 * hh + 64)
                        zp, zs = ps[:, 4 + hh, :], ps[:, 6 + hh, :]
                        mm(zp[:, 0:256], kT[r, 0:128], qT[r, 0:256], True)
                        mm(zp[:, 256:384], kT[r, 128:256], qT[r, 128:256], False)
                        mm(zs[:, 0:64], kT[r, 384:512], qT[r, 256:320], True)
                        mm(zs[:, 64:128], kT[r, 512:640], qT[r, 256:320], False)
                        last = mm(zs[:, 128:192], kT[r, 256:384], qT[r, 256:320], False)
                    last.then_inc(b_z, 1)
                if P_on:
                    if not first:
                        pe.wait_ge(b_k_out, p)
                    for k in range(KD):
                        last = mm3(ps[:, 1, 0:TOK], w_hi[j][:, k, P:2 * P], w_lo[j][:, k, P:2 * P],
                                   hT_hi[:, k, 0:TOK], hT_lo[:, k, 0:TOK], k == 0, k == KD - 1)
                    last.then_inc(b_k, 1)
                if z_on:
                    for t in range(TILES):
                        last = nc.tensor.transpose(ps[:, 2, t * P:(t + 1) * P], b_kT[jz][:, t * P:(t + 1) * P], ident)
                    last.then_inc(b_tk, 1)
                if P_on:
                    pe.wait_ge(b_q_out, p + 1)
                    for t in range(TILES):
                        sl = slice(t * P, (t + 1) * P)
                        for k in range(KD):
                            last = mm3(ps[:, 0, sl], hT_hi[:, k, sl], hT_lo[:, k, sl],
                                       w_hi[j][:, k, 2 * P:3 * P], w_lo[j][:, k, 2 * P:3 * P], k == 0, k == KD - 1)
                    last.then_inc(b_vp, 1)
                    pe.drain()
                    pe.nop().then_inc(unit_used, 1)
                if z_on:
                    pe.wait_ge(b_spm, p)
                    for hh in range(2):
                        zp, zs = ps[:, 4 + hh, :], ps[:, 6 + hh, :]
                        a, s = z_sp[0][:, hh, :], z_sp[1][:, hh, :]
                        mm(zp[:, 0:384], tri_neg, a, False)
                        mm(zp[:, 128:256], ones_neg[:], a[:, 256:384], False)
                        mm(zs[:, 0:192], tri_neg, s, False)
                        mm(zs[:, 0:64], ones_neg[:], s[:, 64:128], False)
                        mm(zs[:, 0:64], ones_neg[:], s[:, 128:192], False)
                        last = mm(zs[:, 64:128], ones_neg[:], s[:, 128:192], False)
                    last.then_inc(b_c, 1)
                if P_on:
                    if z_on:
                        pe.wait_ge(b_tk_out, p)
                    pe.wait_ge(b_cache[j], cache_value)
                    for n in range(2):
                        last = nc.tensor.transpose(ps[:, 2, n * P:(n + 1) * P], b_kc[j][:, n, :], ident)
                    last.then_inc(b_tc, 1)

            b_iteration(0, 0, True, False, False, True, 32)
            b_iteration(1, 1, True, True, False, False, 32)
            with pe.Fori(1, 4) as i:
                for j in range(2):
                    b_iteration(2 * i + j, j, True, True, True, False, 32 * (i + 1))
            b_iteration(8, 0, False, True, True, False, 0)
            b_iteration(9, 1, False, False, True, False, 0)

            pe.wait_ge(mod_ready, 2)
            first_mix[0] = 8
            pe.wait_ge(b_olo, 8)
            pe.wait_ge(b_v_out, 8)
            pe.wait_ge(b_k_out, 8)
            pe.wait_ge(b_tk_out, 8)
            pe.wait_ge(b_tc_out, 8)
            mix(0, S_MIXB, True)
            with pe.Fori(1, 4) as c:
                mix(c, S_MIXB, False)

            pe.wait_ge(x_mix, 16)
            for n, col in enumerate((16, 40)):
                for s in range(2):
                    if n:
                        pe.wait_ge(gb_ready, s + 1)
                    for k in range(KD):
                        last = mm(ps[:, 4 + 2 * s + k // 4, (k % 4) * P:(k % 4 + 1) * P],
                                  mod[:, col + k, s:s + 1].broadcast_to([P, P]), ident, k % 4 == 0)
                    last.then_inc(gb_done, 1)

            pe.wait_ge(m_ready, 1)
            for u in range(4):
                pe.wait_ge(split_done, S_OUT + u + 1)
                for t in range(TILES):
                    if u == 1 or u == 2 or u == 3:
                        pe.wait_ge(o_added, 3 * (u - 1) + t + 1)
                    for k in range(KD):
                        sl = slice(t * P, min((t + 1) * P, TOK))
                        last = mm3(ps[0:rows_of(t), t, 0:MIX_COLS], oT_hi[:, k, sl], oT_lo[:, k, sl],
                                   w_hi[u % 2][:, k, 0:MIX_COLS], w_lo[u % 2][:, k, 0:MIX_COLS], k == 0, k == KD - 1)
                    last.then_inc(o_done, 1)
                pe.drain()
                pe.nop().then_inc(unit_used, 1)

            pe.wait_ge(n_scaled, 6)
            pe.wait_ge(gb_ready, 4)
            for k in range(KD - 1):
                rows_to_columns(xn2, k, k).then_inc(n_T, 1)
            pe.wait_ge(n_out_a, 5)
            rows_to_columns(xn2, KD - 1, 0).then_inc(n_T, 1)
            pe.wait_ge(h2_ready, 2)
            pe.wait_ge(router_in, 64)
            for t in range(TILES):
                for k in range(KD):
                    mm(ps[:, 1, t * 36:(t + 1) * 36], xnT[:, k, t * P:(t + 1) * P], rw[:, k, :], k == 0, False)
                last = mm(ps[:, 1, t * 36:(t + 1) * 36], ones[0:1, :], rb[:], False)
            last.then_inc(r_log, 1)
            for t in range(TILES):
                for half in range(2):
                    b = 2 + 2 * t + half if t < 2 else 6 + half
                    for k in range(4):
                        last = nc.tensor.transpose(ps[:, b, k * P:(k + 1) * P], xnT[:, 4 * half + k, t * P:(t + 1) * P], ident)
                    last.then_inc(r_T, 1)
            pe.wait_ge(r_M, 1)
            for t in range(TILES):
                for u in range(t):
                    mm(ps[:, 0, t * EXPERTS:(t + 1) * EXPERTS], ones[:], M[:, u, :], u == 0, False)
                mm(ps[:, 0, t * EXPERTS:(t + 1) * EXPERTS], before, M[:, t, :], t == 0)
            for t in range(TILES):
                last = mm(ps[:, 0, 3 * EXPERTS:4 * EXPERTS], ones[:], M[:, t, :], t == 0, t == 2)
            last.then_inc(r_rank, 1)

            pe.wait_ge(rounds_ready, 1)
            pe.wait_ge(r_rows, 6)
            rounds = pe.value_load(rnd_i[0:1, 0:1], min_val=1, max_val=MAX_ROUNDS)

            def gather_T(q, n4, n2):
                j = q % 2
                rows, copied = pe.to_reg(16 * (n4 + 1)), pe.to_reg(n2 + 1)
                pe.wait_ge(rounds_ready, 1)
                pe.wait_ge(gathered[q], rows)
                pe.wait_ge(e_xT[j], copied)
                for k in range(KD):
                    last = nc.tensor.transpose(ps[:, j, k * SLOTS:(k + 1) * SLOTS], xg[q][:, k:D:KD], ident[0:SLOTS, 0:SLOTS])
                last.then_inc(e_T[j], 1)

            def hidden(q, n4, n2):
                j = q % 2
                pe.wait_ge(ew_loaded[q], 48 * (n4 + 1))
                pe.wait_ge(e_xT[j], n2 + 2)
                pe.wait_ge(e_hid[j], n2 + 1)
                for w in range(2):
                    for m in range(2):
                        for k in range(KD):
                            c = (2 * w + m) * SLOTS
                            last = mm(ps[:, 2 + j, c:c + SLOTS], ew[q][w][:, k, m:FE:2], xgT[j][:, k, :], k == 0, k == KD - 1)
                last.then_inc(e_h[j], 1)

            def down(q, n4, n2):
                j = q % 2
                pe.wait_ge(e_hid[j], n2 + 2)
                pe.wait_ge(e_out_a[j], n2 + 1)
                pe.wait_ge(e_out_v[j], n2 + 1)
                for half in range(2):
                    for m in range(2):
                        last = mm(ps[0:SLOTS, 4 + 2 * j + half, :], hid[j][:, m, :], ew[q][2][:, m, half * 512:(half + 1) * 512],
                                  m == 0, m == 1)
                last.then_inc(e_y[j], 1)
                pe.drain()
                pe.nop().then_inc(ew_used[q], 1)

            with pe.Fori(0, rounds) as r:
                with pe.Fori(0, 8) as i:
                    n4 = 8 * r + i
                    n2 = 2 * n4
                    gather_T(0, n4, n2)
                    gather_T(1, n4, n2)
                    hidden(0, n4, n2)
                    gather_T(2, n4, n2 + 1)
                    hidden(1, n4, n2)
                    down(0, n4, n2)
                    gather_T(3, n4, n2 + 1)
                    hidden(2, n4, n2 + 1)
                    down(1, n4, n2)
                    hidden(3, n4, n2 + 1)
                    down(2, n4, n2 + 1)
                    down(3, n4, n2 + 1)


        @block.scalar
        def _(act):
            A = nc.scalar.activation
            nc.scalar.preload_act_table_set("natural_log_exp_and_others")
            act.wait_ge(small_in, 96)
            A(c_sig[64:80, :], vec_rows[64:80, :], ACT.Exp, scale=-1.0).then_inc(c_act, 1)

            def root(dst, tmp, src, n, done):
                A(tmp, src, ACT.Ln, bias=eps[:, 0:1], scale=1.0 / n)
                act.drain()
                A(dst, tmp, ACT.Exp, scale=-0.5).then_inc(done, 1)

            def norm_rows(scratch):
                for t in range(TILES):
                    A(scratch[:, t, :], x_sb[:, t, :], ACT.Square, accum_out=stat[:, t:t + 1])
                act.drain()
                root(rstd[:], stat_ln[:], stat[:], D, n_rstd)

            def norm_out(n0):
                for k in range(0, KD, 2):
                    act.wait_ge(n_T, n0 + k + 1)
                    A(xnT[:, k, :], ps[:, k, 0:PADDED], ACT.Copy).then_inc(n_out_a, 1)

            act.wait_ge(setup_done, 1)
            act.wait_ge(x_in, 32)
            norm_rows(xn)
            act.wait_ge(lam_dve, 1)
            A(lam_exp[:], lam_sum[:], ACT.Exp).then_inc(lam_act, 1)
            norm_out(0)

            def split(s, j, loaded):
                act.wait_ge(raw_loaded[j], loaded)
                if not (isinstance(s, int) and s < 2):
                    act.wait_ge(unit_used, s - 1)
                A(w_hi[j][:], raw[j][:], ACT.Copy).then_inc(split_hi, 1)

            split(0, 0, 48)
            for n in range(2):
                act.wait_ge(h_full, n + 1)
                A(hT_hi[:, 4 * n:4 * n + 4, :], xnT[:, 4 * n:4 * n + 4, :], ACT.Copy).then_inc(h_hi, 1)

            def a_iteration(h, j, P_on, qk_on, s1_on, o_on, loaded, store_value):
                jq = 1 - j
                if qk_on:
                    act.wait_ge(a_staged, 3 * h)
                    if not (isinstance(h, int) and h == 1):
                        act.wait_ge(a_ss, h - 1)
                    A(sq[:], stage[jq][:, :, 0:256], ACT.Square).then_inc(a_sq, 1)
                    act.wait_ge(a_ss, h)
                    if not (isinstance(h, int) and h == 1):
                        act.wait_ge(a_scaled, h - 1)
                    root(rs[:], ss_ln[:], ss[:], 64, a_rs)
                if loaded is not None:
                    split(h + 1, jq, loaded)

                def stage_out(t):
                    act.wait_ge(a_proj, 3 * h + t + 1)
                    if t == 0:
                        if store_value is not None:
                            act.wait_ge(a_stored[j], store_value)
                            act.wait_ge(a_qkT, h - 1)
                            act.wait_ge(a_vkept, h - 1)
                    A(stage[j][:, t, :], ps[:, t, 0:UNIT], ACT.Copy).then_inc(a_staged, 1)

                if P_on:
                    stage_out(0)
                if o_on:
                    act.wait_ge(a_pv, h - 2)
                    A(osq[:], ps[:, 7, 0:PADDED].rearrange("p (t c) -> p t c", t=TILES), ACT.Square).then_inc(a_osq, 1)
                    act.wait_ge(a_oss, h - 2)
                    root(o_rs[:], o_ln[:], o_ss[:], P, a_ors)
                if s1_on:
                    act.wait_ge(a_max[1], h - 1)
                    for mp in range(2):
                        last = A(probs[mp][:, 384:704], ps[:, 5 + mp, 0:320], ACT.Exp, bias=a_nmx[:, mp, 2:3],
                                 accum_out=a_sum[:, mp, 2:3])
                    last.then_inc(a_exp[1], 1)
                if P_on:
                    stage_out(1)
                if o_on:
                    act.wait_ge(a_oT, h - 2)
                    A(oT_hi[:, bass.ds(h - 3, 1), :].rearrange("p a n -> p (a n)"), ps[:, 4, 0:TOK], ACT.Copy,
                      scale=subln[:, 0:1]).then_inc(a_ohi, 1)
                if qk_on:
                    act.wait_ge(a_qkT, h)
                    A(qkT[:, 0:512], ps[:, 3, :], ACT.Copy).then_inc(a_qkT_act, 1)
                if P_on:
                    stage_out(2)
                if s1_on:
                    act.wait_ge(a_aT, h - 1)
                    A(aT[:, 0:512], ps[:, 3, :], ACT.Copy).then_inc(a_aT_act, 1)
                if qk_on:
                    act.wait_ge(a_max[0], h)
                    for mp in range(2):
                        for t, sl in ((0, slice(0, 128)), (1, slice(128, 384))):
                            last = A(probs[mp][:, sl], ps[:, 5 + mp, sl], ACT.Exp, bias=a_nmx[:, mp, t:t + 1],
                                     accum_out=a_sum[:, mp, t:t + 1])
                    last.then_inc(a_exp[0], 1)

            for h in range(4):
                a_iteration(h, h % 2, True, h >= 1, h >= 2, h >= 3, 48 * ((h + 1) // 2 + 1), 64 * (h // 2) if h >= 2 else None)
            with act.Fori(2, 4) as i:
                for j in range(2):
                    a_iteration(2 * i + j, j, True, True, True, True, 48 * (i + 1 + j), 64 * i)
            for h in range(8, 11):
                a_iteration(h, h % 2, False, h < 9, h < 10, True, 48 * 5 if h == 8 else None, None)

            def mix(c, s0, n0, next_loaded, first):
                for m in range(2):
                    act.wait_ge(x_g, n0 + c + 1)
                    if not first:
                        act.wait_ge(x_mix, 2 * n0 + 2 * c - 1 + m)
                    A(sig[m][:], ps[:, m, 0:TOK], ACT.Exp, scale=-1.0).then_inc(x_e, 1)
                if next_loaded is not None:
                    for j in range(2):
                        split(s0 + 2 * c + 2 + j, j, next_loaded)

            act.wait_ge(a_comb, 16)
            mix(0, S_MIXA, 0, 48 * 6, True)
            with act.Fori(1, 3) as c:
                mix(c, S_MIXA, 0, 48 * (c + 6), False)
            mix(3, S_MIXA, 0, None, False)
            split(S_B, 0, 48 * 9)

            def b_iteration(p, j, P_on, z_on, w_on, loaded):
                if w_on:
                    act.wait_ge(b_c, p - 1)
                    if not (isinstance(p, int) and p == 2):
                        act.wait_ge(b_o, p - 2)
                    A(z_w[0][:], ps[:, 4:6, 0:384], ACT.Exp)
                    A(z_w[1][:], ps[:, 6:8, 0:192], ACT.Exp).then_inc(b_w, 1)
                if P_on:
                    act.wait_ge(b_q, p + 1)
                    A(b_qT[j][:], ps[:, 0, 0:TOK], ACT.Copy, scale=0.125).then_inc(b_q_out, 1)
                if w_on:
                    act.wait_ge(b_o, p - 1)
                    A(oT_hi[:, bass.ds(p - 2, 1), :].rearrange("p a n -> p (a n)"), ps[:, 3, 0:TOK], ACT.Copy).then_inc(b_ohi, 1)
                if loaded is not None:
                    split(S_B + p + 1, 1 - j, loaded)
                if z_on:
                    act.wait_ge(b_z, p)
                    if w_on:
                        act.wait_ge(b_sp, p - 1)
                    A(z_na[0][:], ps[:, 4:6, 0:384], ACT.Abs)
                    A(z_na[1][:], ps[:, 6:8, 0:192], ACT.Abs)
                    act.drain()
                    for f in range(2):
                        A(z_na[f][:], z_na[f][:], ACT.Exp, scale=-1.0)
                    act.drain()
                    for f in range(2):
                        last = A(z_na[f][:], z_na[f][:], ACT.Ln, bias=1.0)
                    last.then_inc(b_l, 1)
                if P_on:
                    act.wait_ge(b_k, p + 1)
                    if w_on:
                        act.wait_ge(b_tk, p - 1)
                    A(b_kT[j][:, 0:TOK], ps[:, 1, 0:TOK], ACT.Copy).then_inc(b_k_out, 1)

            act.wait_ge(x_mix, 8)
            b_iteration(0, 0, True, False, False, 48 * 9)
            b_iteration(1, 1, True, True, False, 48 * 10)
            with act.Fori(1, 3) as i:
                for j in range(2):
                    b_iteration(2 * i + j, j, True, True, True, 48 * (i + 9 + j))
            b_iteration(6, 0, True, True, True, 48 * 12)
            b_iteration(7, 1, True, True, True, None)
            b_iteration(8, 0, False, True, True, None)
            b_iteration(9, 1, False, False, True, None)
            split(S_MIXB, 0, 48 * 13)
            split(S_MIXB + 1, 1, 48 * 13)
            mix(0, S_MIXB, 4, 48 * 14, True)
            with act.Fori(1, 4) as c:
                mix(c, S_MIXB, 4, 48 * (c + 14), False)

            for s in range(2):
                act.wait_ge(gb_done, s + 1)
                A(g1b[:, s, :], ps[:, 4 + 2 * s:6 + 2 * s, :], ACT.Copy).then_inc(gb_ready, 1)
            for s in range(2):
                act.wait_ge(gb_done, s + 3)
                A(g2b[:, s, :], ps[:, 4 + 2 * s:6 + 2 * s, :], ACT.Copy).then_inc(gb_ready, 1)
            act.wait_ge(x_mix, 16)
            A(oT_hi[:], xnT[:, :, 0:TOK], ACT.Copy).then_inc(m_hi, 1)
            split(S_OUT + 2, 0, 48 * 18)
            split(S_OUT + 3, 1, 48 * 18)

            act.wait_ge(o_added, 12)
            norm_rows(xn2)
            norm_out(8)
            act.wait_ge(r_sub, 1)
            A(lsub[:], lsub[:], ACT.Exp).then_inc(r_exp, 1)
            for t in range(TILES):
                act.wait_ge(r_T, 2 * t + 1)
                A(h2tok[:, t, 0:512], ps[:, 2 + 2 * t, :], ACT.Copy).then_inc(r_rows, 1)
            act.wait_ge(r_e2, 1)
            A(e2[:], e2[:], ACT.Exp).then_inc(r_e2x, 1)

            act.wait_ge(rounds_ready, 1)
            for s in e_xT + e_out_a:
                act.nop().then_inc(s, 1)
            rounds = act.value_load(rnd_i[0:1, 0:1], min_val=1, max_val=MAX_ROUNDS)

            def columns_out(q, n2):
                j = q % 2
                act.wait_ge(e_T[j], n2 + 2)
                act.wait_ge(e_h[j], n2 + 1)
                A(xgT[j][:], ps[:, j, :].rearrange("p (k s) -> p k s", k=KD), ACT.Copy).then_inc(e_xT[j], 1)

            def expo(q, n2):
                j = q % 2
                act.wait_ge(e_h[j], n2 + 2)
                act.wait_ge(e_hid[j], n2 + 1)
                A(h_e[j][:], ps[:, 2 + j, 0:2 * SLOTS], ACT.Exp, scale=-1.0).then_inc(e_exp[j], 1)

            def rows_out(q, n2, r, e):
                j = q % 2
                act.wait_ge(e_y[j], n2 + 2)
                act.wait_ge(y_stored[j], 16 * n2 + 16)
                A(y_sb[j][:, 0:512], ps[0:SLOTS, 4 + 2 * j, :], ACT.Copy,
                  scale=tab[:, bass.ds(e, 1), 2:3].rearrange("p a b -> p (a b)")).then_inc(e_out_a[j], 1)

            with act.Fori(0, rounds) as r:
                act.wait_ge(tab_in, 16 * r + 16)
                with act.Fori(0, 8) as i:
                    n2 = 16 * r + 2 * i
                    columns_out(0, n2)
                    columns_out(1, n2)
                    expo(0, n2)
                    columns_out(2, n2 + 1)
                    expo(1, n2)
                    rows_out(0, n2, r, 4 * i)
                    columns_out(3, n2 + 1)
                    expo(2, n2 + 1)
                    rows_out(1, n2, r, 4 * i + 1)
                    expo(3, n2 + 1)
                    rows_out(2, n2 + 1, r, 4 * i + 2)
                    rows_out(3, n2 + 1, r, 4 * i + 3)

        @block.vector
        def _(dve):
            V = nc.vector
            dve.wait_ge(c_act, 1)
            V.tensor_scalar(c_sig[64:80, :], c_sig[64:80, :], 1.0, None, ALU.add)
            dve.drain()
            V.reciprocal(c_sig[64:80, :], c_sig[64:80, :])
            dve.drain()
            V.tensor_tensor(vec_rows[64:80, :], vec_rows[64:80, :], c_sig[64:80, :], ALU.mult).then_inc(c_dve, 1)
            dve.wait_ge(vecT_done, 1)
            V.tensor_copy(vec_cols[:], ps[:, 0, 0:80]).then_inc(vec_ready, 1)
            dve.drain()

            dve.wait_ge(rows_in, 144)
            for n in range(2):
                V.tensor_tensor(lam_prod[:, n, :], lam_rows[:, 2 * n, :], lam_rows[:, 2 * n + 1, :], ALU.mult)
            V.tensor_scalar(gqk[:, 0:2, :], gqk[:, 0:2, :], 0.125, None, ALU.mult)
            V.tensor_scalar(subln[:], subln[:], 1.0 - LAM_INIT, None, ALU.mult)
            dve.drain()
            V.tensor_reduce(lam_sum[:], lam_prod[:], AX, ALU.add).then_inc(lam_dve, 1)

            def scale_rows(dst, n0):
                dve.wait_ge(n_rstd, n0)
                for t in range(TILES):
                    V.tensor_scalar(dst[:, t, :], x_sb[:, t, :], rstd[:, t:t + 1], None, ALU.mult).then_inc(n_scaled, 1)

            def norm_out(n0):
                for k in range(1, KD, 2):
                    dve.wait_ge(n_T, n0 + k + 1)
                    V.tensor_copy(xnT[:, k, :], ps[:, 0 if k == KD - 1 else k, 0:PADDED]).then_inc(n_out_v, 1)

            def modulate(gain, shift, n0, done):
                dve.wait_ge(n_out_a, n0)
                dve.wait_ge(n_out_v, n0)
                for k in range(KD):
                    for s, sl in ((0, slice(0, SEQ)), (1, slice(SEQ, TOK))):
                        last = V.tensor_scalar(xnT[:, k, sl], xnT[:, k, sl], gain[:, k, s:s + 1],
                                               mod[:, shift + k, s:s + 1], ALU.mult, ALU.add)
                    if k % 4 == 3:
                        last.then_inc(done, 1)

            def mod_columns(lo, hi, column, gain, scale_at, norm_at):
                n = hi - lo
                V.tensor_tensor(mod[:, lo:hi, :], ps[:, 7, column:column + 2 * n].rearrange("p (n s) -> p n s", s=2),
                                vec_cols[:, lo:hi].unsqueeze(2).broadcast_to([P, n, 2]), ALU.add)
                dve.drain()
                V.scalar_tensor_tensor(gain[:], mod[:, scale_at:scale_at + KD, :], 1.0,
                                       vec_cols[:, norm_at:norm_at + KD].unsqueeze(2).broadcast_to([P, KD, 2]),
                                       ALU.add, ALU.mult).then_inc(mod_ready, 1)
                dve.drain()

            scale_rows(xn, 1)
            dve.wait_ge(lam_act, 1)
            V.tensor_tensor(neg_lam[:], lam_exp[:, 1:2], lam_exp[:, 0:1], ALU.subtract)
            dve.drain()
            V.tensor_scalar(neg_lam[:], neg_lam[:], -LAM_INIT, None, ALU.add)
            norm_out(0)

            def split(s, j):
                dve.wait_ge(split_hi, s + 1)
                V.tensor_tensor(w_lo[j][:], raw[j][:], f32(w_hi[j][:]), ALU.subtract).then_inc(split_done, 1)

            split(0, 0)
            dve.wait_ge(ada_used, 8)
            mod_columns(0, 16, 0, gain1, 8, 48)
            modulate(gain1, 0, 4, h_full)
            for n in range(2):
                ks = slice(4 * n, 4 * n + 4)
                dve.wait_ge(h_hi, n + 1)
                V.tensor_tensor(hT_lo[:, ks, :], xnT[:, ks, :], f32(hT_hi[:, ks, :]), ALU.subtract).then_inc(h_ready, 1)


            def combine(parts, f):
                V.reciprocal(a_rec[:, :, parts[0][0]:parts[-1][0] + 1], a_sum[:, :, parts[0][0]:parts[-1][0] + 1])
                dve.drain()
                V.tensor_scalar(a_rec[:, 1, parts[0][0]:parts[-1][0] + 1], a_rec[:, 1, parts[0][0]:parts[-1][0] + 1],
                                neg_lam[:, 0:1], None, ALU.mult)
                for t, sl in parts:
                    V.tensor_scalar(amap[:, sl], probs[0][:, sl], a_rec[:, 0, t:t + 1], None, ALU.mult)
                dve.drain()
                for t, sl in parts:
                    last = V.scalar_tensor_tensor(amap[:, sl], probs[1][:, sl], a_rec[:, 1, t:t + 1], amap[:, sl],
                                                  ALU.mult, ALU.add)
                last.then_inc(a_comb, 1)

            def a_iteration(h, j, qk_on, s1_on, o_on, split_on):
                jq = 1 - j
                if qk_on:
                    dve.wait_ge(a_sq, h)
                    V.tensor_reduce(ss[:].rearrange("p (t n) -> p t n", t=TILES),
                                    sq[:].rearrange("p t (n c) -> p t n c", n=4), AX, ALU.add).then_inc(a_ss, 1)
                    dve.wait_ge(a_rs, h)
                    st = stage[jq][:, :, 0:256].rearrange("p t (n c) -> p t n c", n=4)
                    V.tensor_tensor(st, st, rs[:].rearrange("p (t n) -> p t n", t=TILES).unsqueeze(3).broadcast_to([P, TILES, 4, 64]),
                                    ALU.mult).then_inc(a_scaled, 1)
                if o_on:
                    dve.wait_ge(a_osq, h - 2)
                    V.tensor_reduce(o_ss[:], osq[:], AX, ALU.add).then_inc(a_oss, 1)
                    dve.wait_ge(a_ors, h - 2)
                    if not (isinstance(h, int) and h == 3):
                        dve.wait_ge(a_oT, h - 3)
                    V.tensor_tensor(o_n[:], ps[:, 7, 0:PADDED].rearrange("p (t c) -> p t c", t=TILES),
                                    o_rs[:].unsqueeze(2).broadcast_to([P, TILES, P]), ALU.mult).then_inc(a_on, 1)
                if s1_on:
                    dve.wait_ge(a_s[1], h - 1)
                    V.tensor_reduce(a_mx[:, :, 2:3], ps[:, 5:7, 0:320], AX, ALU.max)
                    dve.drain()
                    V.tensor_scalar(a_nmx[:, :, 2:3], a_mx[:, :, 2:3], -1.0, None, ALU.mult).then_inc(a_max[1], 1)
                    dve.wait_ge(a_exp[1], h - 1)
                    combine([(2, slice(384, 704))], 1)
                if o_on:
                    dve.wait_ge(a_ohi, h - 2)
                    dst = lambda x: x[:, bass.ds(h - 3, 1), :].rearrange("p a n -> p (a n)")
                    V.scalar_tensor_tensor(dst(oT_lo), ps[:, 4, 0:TOK], subln[:, 0:1], f32(dst(oT_hi)),
                                           ALU.mult, ALU.subtract).then_inc(a_olo, 1)
                if qk_on:
                    dve.wait_ge(a_qkT, h)
                    V.tensor_copy(qkT[:, 512:1024], ps[:, 4, :]).then_inc(a_qkT_dve, 1)
                if split_on:
                    split(h + 1, jq)
                if s1_on:
                    dve.wait_ge(a_aT, h - 1)
                    V.tensor_copy(aT[:, 512:768], ps[:, 4, 0:256]).then_inc(a_aT_dve, 1)
                if qk_on:
                    dve.wait_ge(a_s[0], h)
                    V.memset(ps[0:64, 5:7, :].rearrange("p b (u c) -> p b u c", u=2)[:, :, :, 64:128], NEG)
                    dve.drain()
                    V.tensor_reduce(a_mx[:, :, 0:1], ps[:, 5:7, 0:128], AX, ALU.max)
                    V.tensor_reduce(a_mx[:, :, 1:2], ps[:, 5:7, 128:384], AX, ALU.max)
                    dve.drain()
                    V.tensor_scalar(a_nmx[:, :, 0:2], a_mx[:, :, 0:2], -1.0, None, ALU.mult).then_inc(a_max[0], 1)
                    dve.wait_ge(a_exp[0], h)
                    combine([(0, slice(0, 128)), (1, slice(128, 384))], 0)

            dve.wait_ge(setup_done, 1)
            for h in range(4):
                a_iteration(h, h % 2, h >= 1, h >= 2, h >= 3, True)
            with dve.Fori(2, 4) as i:
                for j in range(2):
                    a_iteration(2 * i + j, j, True, True, True, True)
            for h in range(8, 11):
                a_iteration(h, h % 2, h < 9, h < 10, True, h == 8)

            def mix(c, s0, n0, split_next):
                for m in range(2):
                    n = 2 * n0 + 2 * c + m
                    dve.wait_ge(x_e, n + 1)
                    V.tensor_scalar(sig[m][:], sig[m][:], 1.0, None, ALU.add)
                    dve.drain()
                    V.reciprocal(sig_r[m][:], sig[m][:])
                dve.drain()
                dve.wait_ge(x_o, n0 + c + 1)
                for m in range(2):
                    dst = xnT[:, bass.ds(2 * c + m, 1), 0:TOK].rearrange("p a n -> p (a n)")
                    if n0:
                        V.tensor_tensor(sig_r[m][:], sig_r[m][:], ps[:, 2 + m, 0:TOK], ALU.mult)
                        dve.drain()
                        V.tensor_tensor(dst, dst, sig_r[m][:], ALU.add).then_inc(x_mix, 1)
                    else:
                        V.tensor_tensor(dst, sig_r[m][:], ps[:, 2 + m, 0:TOK], ALU.mult).then_inc(x_mix, 1)
                if split_next:
                    for j in range(2):
                        split(s0 + 2 * c + 2 + j, j)

            mix(0, S_MIXA, 0, True)
            with dve.Fori(1, 3) as c:
                mix(c, S_MIXA, 0, True)
            mix(3, S_MIXA, 0, False)
            split(S_B, 0)
            dve.wait_ge(late_used, 16)
            mod_columns(16, 48, 384, gain2, 32, 56)

            def b_iteration(p, j, P_on, z_on, w_on, split_on, store_v, store_k):
                jz = 1 - j
                if w_on:
                    dve.wait_ge(b_ohi, p - 1)
                    dst = lambda x: x[:, bass.ds(p - 2, 1), :].rearrange("p a n -> p (a n)")
                    V.tensor_tensor(dst(oT_lo), ps[:, 3, 0:TOK], f32(dst(oT_hi)), ALU.subtract).then_inc(b_olo, 1)
                if split_on:
                    split(S_B + p + 1, jz)
                if z_on:
                    dve.wait_ge(b_l, p)
                    if w_on:
                        dve.wait_ge(b_c, p - 1)
                    V.scalar_tensor_tensor(z_sp[0][:], ps[:, 4:6, 0:384], 0.0, z_na[0][:], ALU.max, ALU.add)
                    V.scalar_tensor_tensor(z_sp[1][:], ps[:, 6:8, 0:192], 0.0, z_na[1][:], ALU.max, ALU.add).then_inc(b_sp, 1)
                    dve.wait_ge(b_tk, p)
                    if store_k is not None:
                        dve.wait_ge(b_stored[jz], store_k)
                    V.tensor_copy(b_ktok[jz][:], ps[:, 2, 0:PADDED].rearrange("p (t c) -> p t c", t=TILES)).then_inc(b_tk_out, 1)
                if P_on:
                    dve.wait_ge(b_vp, p + 1)
                    if store_v is not None:
                        dve.wait_ge(b_stored[j], store_v)
                        dve.wait_ge(b_o, p - 1)
                    V.tensor_copy(b_v[j][:], ps[:, 0, 0:PADDED].rearrange("p (t c) -> p t c", t=TILES)).then_inc(b_v_out, 1)
                    dve.wait_ge(b_tc, p + 1)
                    V.tensor_copy(b_kT[j][:, 384:640], ps[:, 2, 0:256]).then_inc(b_tc_out, 1)

            b_iteration(0, 0, True, False, False, True, None, None)
            b_iteration(1, 1, True, True, False, True, None, None)
            with dve.Fori(1, 3) as i:
                for j in range(2):
                    b_iteration(2 * i + j, j, True, True, True, True, 64 * i, 64 * (i - 1 + j))
            for j in range(2):
                b_iteration(6 + j, j, True, True, True, j == 0, 64 * 3, 64 * (2 + j))
            b_iteration(8, 0, False, True, True, False, None, 64 * 3)
            b_iteration(9, 1, False, False, True, False, None, None)
            split(S_MIXB, 0)
            split(S_MIXB + 1, 1)
            mix(0, S_MIXB, 4, True)
            with dve.Fori(1, 4) as c:
                mix(c, S_MIXB, 4, True)

            dve.wait_ge(m_hi, 1)
            V.tensor_tensor(oT_lo[:], xnT[:, :, 0:TOK], f32(oT_hi[:]), ALU.subtract).then_inc(m_ready, 1)
            for u in range(4):
                for t in range(TILES):
                    n, r = 3 * u + t, rows_of(t)
                    dve.wait_ge(o_done, n + 1)
                    dve.wait_ge(gb_ready, 2)
                    sl = slice(u * MIX_COLS, (u + 1) * MIX_COLS)
                    V.tensor_tensor(wtmp[0:r, t, :], ps[0:r, t, 0:MIX_COLS], g1b[0:r, t // 2, sl], ALU.mult)
                    dve.drain()
                    V.tensor_tensor(x_sb[0:r, t, sl], x_sb[0:r, t, sl], wtmp[0:r, t, :], ALU.add).then_inc(o_added, 1)
                if u < 2:
                    split(S_OUT + 2 + u, u)
            dve.drain()

            scale_rows(xn2, 2)
            norm_out(8)
            modulate(gain2, 24, 8, h2_ready)

            def bc(a, n):
                return a.unsqueeze(len(a.shape)).broadcast_to(list(a.shape) + [n])

            def row(a, n):
                return cst[:, a:a + n].unsqueeze(1).broadcast_to([P, TILES, n])

            def tt(out, a, b, op):
                ins = V.tensor_tensor(out, a, b, op)
                dve.drain()
                return ins

            def red(out, a, op):
                ins = V.tensor_reduce(out, a, AX, op)
                dve.drain()
                return ins

            dve.wait_ge(r_log, 1)
            V.tensor_copy(lg[:], ps[:, 1, 0:108].rearrange("p (t n) -> p t n", t=TILES))
            dve.drain()
            red(gmax[:], lg[:, :, 0:4], ALU.max)
            V.tensor_tensor(lsub[:], lg[:, :, 0:4], bc(gmax[:], 4), ALU.subtract).then_inc(r_sub, 1)
            tt(gtie[:], lg[:, :, 0:4], bc(gmax[:], 4), ALU.is_equal)
            tt(gtie[:], gtie[:], row(C_W4, 4), ALU.mult)
            red(gtm[:], gtie[:], ALU.max)
            tt(g1h[:], gtie[:], bc(gtm[:], 4), ALU.is_equal)
            tt(lsel4[:], lg[:, :, 4:36].rearrange("p t (g e) -> p t g e", g=GROUPS), bc(g1h[:], 8), ALU.mult)
            red(lsel[:], lsel4[:].rearrange("p t g e -> p t e g"), ALU.add)
            red(m1[:], lsel[:], ALU.max)
            tt(etie[:], lsel[:], bc(m1[:], 8), ALU.is_equal)
            tt(etie[:], etie[:], row(C_W8, 8), ALU.mult)
            red(etm[:], etie[:], ALU.max)
            tt(eh1[:], etie[:], bc(etm[:], 8), ALU.is_equal)
            V.scalar_tensor_tensor(lsel[:], eh1[:], NEG, lsel[:], ALU.mult, ALU.add)
            dve.drain()
            red(m2[:], lsel[:], ALU.max)
            tt(etie[:], lsel[:], bc(m2[:], 8), ALU.is_equal)
            tt(etie[:], etie[:], row(C_W8, 8), ALU.mult)
            red(etm[:], etie[:], ALU.max)
            tt(eh2[:], etie[:], bc(etm[:], 8), ALU.is_equal)
            V.tensor_tensor(e2[:], m2[:], m1[:], ALU.subtract).then_inc(r_e2, 1)
            for n, eh in enumerate((eh1, eh2)):
                dst = E1[n][:].rearrange("p t (g e) -> p t g e", g=GROUPS)
                V.tensor_tensor(dst, bc(g1h[:], 8), eh[:].unsqueeze(2).broadcast_to([P, TILES, GROUPS, 8]), ALU.mult)
            dve.drain()
            tt(M[:], E1[0][:], E1[1][:], ALU.add)
            V.memset(M[DEC:P, 2, :], 0.0).then_inc(r_M, 1)
            for t in range(TILES):
                dve.wait_ge(r_T, 2 * t + 2)
                V.tensor_copy(h2tok[:, t, 512:1024], ps[:, 3 + 2 * t, :]).then_inc(r_rows, 1)
            dve.wait_ge(r_exp, 1)
            red(pgsum[:], lsub[:], ALU.add)
            V.reciprocal(pg[:], pgsum[:])
            dve.wait_ge(r_e2x, 1)
            V.tensor_scalar(wsum[:], e2[:], 1.0, None, ALU.add)
            dve.drain()
            V.reciprocal(wsum[:], wsum[:])
            dve.drain()
            for n in range(2):
                V.tensor_copy(pair[n][:, :, 0:1], cst[:, C_TOK:C_TOK + 3].unsqueeze(2))
                V.tensor_scalar(pair[n][:, :, 1:2], cst[:, C_TOK:C_TOK + 3].unsqueeze(2), float(1 + n * TOK), None, ALU.add)
            V.tensor_tensor(pair[0][:, :, 2:3], pg[:].unsqueeze(2), wsum[:].unsqueeze(2), ALU.mult)
            dve.drain()
            V.tensor_tensor(pair[1][:, :, 2:3], pair[0][:, :, 2:3], e2[:].unsqueeze(2), ALU.mult)
            dve.wait_ge(r_rank, 1)
            V.scalar_tensor_tensor(rank[:], ps[:, 0, 0:96].rearrange("p (t e) -> p t e", t=TILES), float(EXPERTS),
                                   row(C_E, EXPERTS), ALU.mult, ALU.add)
            V.tensor_reduce(cnt[:], ps[:, 0, 96:128], AX, ALU.max)
            dve.drain()
            for n in range(2):
                tt(rtmp[:], E1[n][:], rank[:], ALU.mult)
                red(posf[:, n, :], rtmp[:], ALU.add)
            V.tensor_copy(posi[:], posf[:]).then_inc(r_pos, 1)
            V.tensor_scalar(thr[:], cst[:, C_THR:C_THR + MAX_ROUNDS], cnt[:, 0:1], None, ALU.is_lt)
            dve.drain()
            red(rnd[:], thr[:], ALU.add)
            V.tensor_copy(rnd_i[:], rnd[:])
            dve.drain()
            dve.nop().then_inc(rounds_ready, 1)
            for s in e_hid + e_out_v:
                dve.nop().then_inc(s, 1)
            rounds = dve.value_load(rnd_i[0:1, 0:1], min_val=1, max_val=MAX_ROUNDS)

            def swiglu(q, n2):
                j = q % 2
                dve.wait_ge(e_exp[j], n2 + 1)
                V.tensor_scalar(h_s[j][:], h_e[j][:], 1.0, None, ALU.add)
                dve.drain()
                V.reciprocal(h_s[j][:], h_s[j][:])
                dve.drain()
                V.tensor_tensor(h_s[j][:], h_s[j][:], ps[:, 2 + j, 0:2 * SLOTS], ALU.mult)
                dve.drain()
                dve.wait_ge(e_y[j], n2 + 1)
                V.tensor_tensor(hid[j][:].rearrange("p m s -> p (m s)"), h_s[j][:], ps[:, 2 + j, 2 * SLOTS:4 * SLOTS],
                                ALU.mult).then_inc(e_hid[j], 1)

            def rows_out(q, n2, e):
                j = q % 2
                dve.wait_ge(e_y[j], n2 + 2)
                dve.wait_ge(y_stored[j], 16 * n2 + 16)
                V.tensor_scalar(y_sb[j][:, 512:1024], ps[0:SLOTS, 5 + 2 * j, :],
                                tab[:, bass.ds(e, 1), 2:3].rearrange("p a b -> p (a b)"), None, ALU.mult).then_inc(e_out_v[j], 1)

            with dve.Fori(0, rounds) as r:
                dve.wait_ge(tab_in, 16 * r + 16)
                V.tensor_copy(tab_i[:], tab[:, :, 0:2]).then_inc(tab_ready, 1)
                with dve.Fori(0, 8) as i:
                    n2 = 16 * r + 2 * i
                    swiglu(0, n2)
                    swiglu(1, n2)
                    rows_out(0, n2, 4 * i)
                    swiglu(2, n2 + 1)
                    rows_out(1, n2, 4 * i + 1)
                    swiglu(3, n2 + 1)
                    rows_out(2, n2 + 1, 4 * i + 2)
                    rows_out(3, n2 + 1, 4 * i + 3)

            dve.wait_ge(back, 64)
            for t in range(TILES):
                r = rows_of(t)
                V.tensor_tensor(ya[0:r, t, :], ya[0:r, t, :], yb[0:r, t, :], ALU.add)
            dve.drain()
            for t in range(TILES):
                r = rows_of(t)
                V.tensor_tensor(ya[0:r, t, :], ya[0:r, t, :], g2b[0:r, t // 2, :], ALU.mult)
            dve.drain()
            for t in range(TILES):
                r = rows_of(t)
                V.tensor_tensor(x_sb[0:r, t, :], x_sb[0:r, t, :], ya[0:r, t, :], ALU.add)
            dve.drain()
            dve.nop().then_inc(y_done, 2)

        @block.gpsimd
        def _(pool):
            G = nc.gpsimd
            G.memset(zero[:], 0.0).then_inc(zero_ready, 1)
            G.memset(ones[:], 1.0)
            G.memset(ones_neg[:], -1.0)
            G.memset(eps[:], EPS)
            pool.drain()
            G.memset(x_sb[DEC:P, 2, :], 0.0)
            pool.drain()
            G.memset(amap[:, 704:768], 0.0)
            pool.drain()
            pool.nop().then_inc(setup_done, 1)

            def rope(m, j, v_free):
                pool.wait_ge(a_scaled, m + 1)
                st = stage[j]
                G.tensor_tensor(st[:, :, 0:256], st[:, :, 0:256],
                                gqk[:].rearrange("p n c -> p (n c)").unsqueeze(1).broadcast_to([P, TILES, 256]), ALU.mult)
                pool.drain()
                x16 = st[:, :, 0:256].rearrange("p t (n c) -> p t n c", n=4)[:, :, :, 0:16]
                cos = cst[:, C_ROPEC:C_ROPEC + 48].rearrange("p (t c) -> p t c", t=TILES)
                sin = cst[:, C_ROPES:C_ROPES + 48].rearrange("p (t c) -> p t c", t=TILES)

                def over_heads(a, lo, hi):
                    return a[:, :, lo:hi].unsqueeze(2).broadcast_to([P, TILES, 4, hi - lo])

                G.tensor_tensor(rope_x[:], x16, over_heads(cos, 0, 16), ALU.mult)
                G.tensor_tensor(rope_y[:, :, :, 0:8], x16[:, :, :, 8:16], over_heads(sin, 0, 8), ALU.mult)
                G.tensor_tensor(rope_y[:, :, :, 8:16], x16[:, :, :, 0:8], over_heads(sin, 8, 16), ALU.mult)
                pool.drain()
                G.tensor_tensor(x16, rope_x[:], rope_y[:], ALU.add).then_inc(a_roped, 1)
                if v_free is not None:
                    before = pool.to_reg(v_free)
                    pool.wait_ge(setup_done, 1)
                    pool.wait_ge(a_pv, before)
                G.tensor_copy(v_keep[j][:], st[:, :, 256:384]).then_inc(a_vkept, 1)
                pool.drain()

            for m in range(2):
                rope(m, m, None)
            with pool.Fori(1, 4) as i:
                for j in range(2):
                    rope(2 * i + j, j, 2 * i + j - 1)

            pool.wait_ge(a_olo, 8)
            pool.wait_ge(x_mix, 8)
            for j in range(2):
                G.memset(b_kT[j][:, TOK:PADDED], 0.0)
            pool.drain()
            pool.nop().then_inc(b_zero, 1)

            def causal(bufs, done):
                for hh in range(2):
                    blocks = bufs[0][:, hh, :].rearrange("p (u c) -> p u c", c=P)[:, 0:3:2, :]
                    G.affine_select(out=blocks, in_=blocks, pattern=[[0, 2], [1, P]], compare_op=ALU.is_gt, fill=0.0,
                                    base=0, channel_multiplier=-1)
                blocks = bufs[1][:, :, P:P + DEC]
                G.affine_select(out=blocks, in_=blocks, pattern=[[0, 2], [1, DEC]], compare_op=ALU.is_gt, fill=0.0,
                                base=0, channel_multiplier=-1).then_inc(done, 1)

            pool.wait_ge(b_sp, 1)
            causal(z_sp, b_spm)
            with pool.Fori(1, 8) as m:
                pool.wait_ge(setup_done, 1)
                pool.wait_ge(b_w, m)
                causal(z_w, b_wm)
                logits = pool.to_reg(m + 1)
                pool.wait_ge(setup_done, 1)
                pool.wait_ge(b_sp, logits)
                causal(z_sp, b_spm)
            pool.wait_ge(b_w, 8)
            causal(z_w, b_wm)

            pool.wait_ge(r_rows, 6)
            for j, ts in enumerate((slice(0, 2), slice(2, 3))):
                pool.dma_start(h2_dram.rearrange("(t p) d -> p t d", p=P)[:, ts, :], h2tok[:, ts, :]).then_inc(y_stored[j], 16)
            pool.wait_ge(r_pos, 1)
            pool.wait_ge(tab_zero, 16)
            for n in range(2):
                for t in range(TILES):
                    r = rows_of(t)
                    G.indirect_dma_start(tab_dram, bass.IndirectOffsetOnAxis(ap=posi[0:r, n, t:t + 1], axis=0),
                                         pair[n][0:r, t, :], None).then_inc(tab_put, 16)
            pool.wait_ge(tab_put, 96)
            for j in range(2):
                pool.wait_ge(y_stored[j], 16)
            pool.wait_ge(rounds_ready, 1)
            rounds = pool.value_load(rnd_i[0:1, 0:1], min_val=1, max_val=MAX_ROUNDS)

            def counts(n4):
                plain = [pool.to_reg(2 * n4 + n) for n in range(1, 4)]
                stores = [pool.to_reg(32 * n4 + 16 * n) for n in range(1, 4)]
                return plain, stores

            def gather(q, copied, transposed, e):
                pool.wait_ge(setup_done, 1)
                pool.wait_ge(e_T[q % 2], transposed)
                G.tensor_copy(idx[q][:], tab_i[:, bass.ds(e, 1), 0:1].rearrange("p a b -> p (a b)")).then_inc(idx_ready[q % 2], 1)
                pool.wait_ge(setup_done, 1)
                pool.wait_ge(idx_ready[q % 2], copied)
                G.indirect_dma_start(xg[q][:], None, h2_dram, bass.IndirectOffsetOnAxis(ap=idx[q][:, 0:1], axis=0)).then_inc(gathered[q], 16)

            def scatter(q, plain, stores, e):
                j, h = q % 2, q // 2
                pool.wait_ge(setup_done, 1)
                pool.wait_ge(e_out_a[j], plain[h + 1])
                pool.wait_ge(e_out_v[j], plain[h + 1])
                G.tensor_copy(row_idx[j][:], tab_i[:, bass.ds(e, 1), 1:2].rearrange("p a b -> p (a b)")).then_inc(row_ready[j], 1)
                pool.wait_ge(setup_done, 1)
                pool.wait_ge(row_ready[j], plain[h])
                pool.wait_ge(y_stored[1 - j], stores[h + j])
                G.indirect_dma_start(y_dram, bass.IndirectOffsetOnAxis(ap=row_idx[j][:, 0:1], axis=0), y_sb[j][:], None).then_inc(y_stored[j], 16)

            with pool.Fori(0, rounds) as r:
                for j in range(2):
                    pool.wait_ge(y_stored[j], 256 * r + 16)
                pool.dma_start(tab[:], tab_dram.rearrange("(s e) a -> s e a", e=EXPERTS)[bass.ds(r * SLOTS, SLOTS)]).then_inc(tab_in, 16)
                after, plain = pool.to_reg(r + 1), [pool.to_reg(16 * r + n) for n in range(1, 3)]
                pool.wait_ge(setup_done, 1)
                pool.wait_ge(tab_ready, after)
                for q in range(4):
                    gather(q, plain[q // 2], plain[0], q)
                for v in [after] + plain:
                    pool.free_register(v)
                with pool.Fori(0, 7) as i:
                    plain, stores = counts(8 * r + i)
                    last_two = pool.to_reg(2 * (8 * r + i) + 4)
                    for q in range(4):
                        scatter(q, plain, stores, 4 * i + q)
                        gather(q, last_two if q // 2 else plain[2], plain[q // 2 + 1], 4 * i + 4 + q)
                    for v in plain + stores + [last_two]:
                        pool.free_register(v)
                plain, stores = counts(8 * r + 7)
                for q in range(4):
                    scatter(q, plain, stores, 28 + q)
            stored_rows = pool.to_reg(256 * rounds + 16)
            pool.wait_ge(setup_done, 1)
            for j in range(2):
                pool.wait_ge(y_stored[j], stored_rows)
            for n, dst in enumerate((ya, yb)):
                first = 1 + n * TOK
                pool.dma_start(dst[:, 0:2, :], y_dram[first:first + SEQ].rearrange("(t p) d -> p t d", p=P)).then_inc(back, 16)
                pool.dma_start(dst[0:DEC, 2, :], y_dram[first + SEQ:first + TOK]).then_inc(back, 16)



_SHAPES = (("y_prompt", (1, SEQ, D)), ("y_sample", (1, DEC, D)),
           ("a_k_prompt", (1, 1, SEQ, 16, 64)), ("a_v_prompt", (1, 1, SEQ, 8, 128)),
           ("b_k_prompt", (1, 1, SEQ, 16, 64)), ("b_v_prompt", (1, 1, SEQ, 16, 64)),
           ("a_k_sample", (1, 1, DEC, 16, 64)), ("a_v_sample", (1, 1, DEC, 8, 128)),
           ("b_k_sample", (1, 1, DEC, 16, 64)), ("b_v_sample", (1, 1, DEC, 16, 64)))


def kernel(**inputs):
    import concourse.bacc as bacc
    from concourse.bass_utils import run_bass_kernel_spmd

    nc = bacc.Bacc("TRN2", target_bir_lowering=False, num_devices=1)
    arrays = {"shape_constants": shape_constants()}
    for name, a in inputs.items():
        a = np.ascontiguousarray(a)
        if name.startswith("cache"):
            a = a.reshape(PAST, D)
        elif not name.startswith(("x_", "c_")):
            a = a.reshape(a.shape[1:])
        arrays[name] = a
    t_in = {name: nc.dram_tensor("in_" + name, a.shape, mybir.dt.from_np(a.dtype), kind="ExternalInput").ap()
            for name, a in arrays.items()}
    t_out = {name: nc.dram_tensor("out_" + name, (shape[-3] * shape[-2] * shape[-1] // D, D) if len(shape) == 5 else shape[1:],
                                  F32, kind="ExternalOutput").ap() for name, shape in _SHAPES}
    build(nc, t_in, t_out)
    r = run_bass_kernel_spmd(nc, [{"in_" + n: a for n, a in arrays.items()}], core_ids=[0])
    return tuple(np.asarray(r.results[0]["out_" + name]).reshape(shape) for name, shape in _SHAPES)
```

```python
from contextlib import ExitStack

import numpy as np

import concourse.bass as bass
from concourse import mybir

P = 128
D = 1024
KD = D // P
SEQ, DEC, PAST = 256, 64, 256
TOK = SEQ + DEC
TILES = 3
PADDED = TILES * P
A_HEADS, B_PAIRS = 8, 8
GROUPS, PER_GROUP = 4, 8
EXPERTS = GROUPS * PER_GROUP
FE = 256
SLOTS = 64
MAX_ROUNDS = TOK // SLOTS
EPS = 1e-6
NEG = -1e30
LAM_INIT = 0.2
ADA_COLS = 256
UNIT = 3 * P
MIX_COLS = 256

ALU = mybir.AluOpType
ACT = mybir.ActivationFunctionType
AX = mybir.AxisListType.X
F32 = mybir.dt.float32
F32R = mybir.dt.float32r
I32 = mybir.dt.int32
U32 = mybir.dt.uint32

C_ID, C_TRI, C_LT, C_ROPEC, C_ROPES = 0, 128, 256, 384, 432
C_TOK, C_THR, C_W4, C_W8, C_E = 480, 483, 488, 492, 500
C_ALL = 532


def shape_constants():
    c = np.zeros((P, C_ALL), np.float32)
    r = np.arange(P)
    c[:, C_ID:C_ID + P] = np.eye(P)
    c[:, C_TRI:C_TRI + P] = -(r[:, None] >= r[None, :]).astype(np.float32)
    c[:, C_LT:C_LT + P] = (r[:, None] < r[None, :]).astype(np.float32)
    half = 8
    inv = np.exp(np.float32(-np.log(500000.0) * 2.0) * np.arange(half, dtype=np.float32) / np.float32(16))
    pos = (np.arange(TILES)[None, :] * P + r[:, None]).astype(np.float32)
    ang = (pos[:, :, None] * inv.astype(np.float32)).astype(np.float32)
    cos, sin = np.cos(ang), np.sin(ang)
    c[:, C_ROPEC:C_ROPEC + 48] = np.concatenate([cos, cos], 2).reshape(P, 48)
    c[:, C_ROPES:C_ROPES + 48] = np.concatenate([-sin, sin], 2).reshape(P, 48)
    c[:, C_TOK:C_TOK + 3] = pos
    c[:, C_THR:C_THR + MAX_ROUNDS] = np.arange(MAX_ROUNDS) * SLOTS
    c[:, C_W4:C_W4 + 4] = 4 - np.arange(4)
    c[:, C_W8:C_W8 + 8] = 8 - np.arange(8)
    c[:, C_E:C_E + 32] = np.arange(32)
    return c


def rows_of(t):
    return P if t < 2 else DEC


def build(nc, t_in, t_out):
    g = t_in
    ctx = ExitStack()
    with ctx:
        def sem(name):
            return ctx.enter_context(nc.semaphore(name))

        top = nc.sbuf_base
        end = top + nc.sbuf_bytes_remaining

        def place(name, shape, dt, at):
            assert at + 4 * int(np.prod(shape[1:])) <= end, name
            return nc.alloc_sbuf_tensor_at(name, shape, dt, offset=at)

        cursor = [(top + 31) // 32 * 32]

        def take(name, shape, dt=F32):
            at = cursor[0]
            cursor[0] += (4 * int(np.prod(shape[1:])) + 31) // 32 * 32
            return place(name, shape, dt, at)

        cst = take("cst", [P, C_ALL])
        ident = cst[:, C_ID:C_ID + P]
        tri_neg = cst[:, C_TRI:C_TRI + P]
        before = cst[:, C_LT:C_LT + P]
        ones = take("ones", [P, P])
        ones_neg = take("ones_neg", [P, P])
        eps = take("eps", [P, 1])
        lam_rows = take("lam_rows", [P, 4, 64])
        lam_prod = take("lam_prod", [P, 2, 64])
        lam_sum = take("lam_sum", [P, 2])
        lam_exp = take("lam_exp", [P, 2])
        neg_lam = take("neg_lam", [P, 1])
        gqk = take("gqk", [P, 4, 64])
        vec_rows = take("vec_rows", [80, P])
        vec_cols = take("vec_cols", [P, 80])
        c_cols = take("c_cols", [P, KD, 32])
        subln = take("subln", [P, 1])
        c_sig = take("c_sig", [80, P])
        mod = take("mod", [P, 48, 2])
        gain1 = take("gain1", [P, KD, 2])
        gain2 = take("gain2", [P, KD, 2])
        stat = take("stat", [P, 3])
        stat_ln = take("stat_ln", [P, 3])
        rstd = take("rstd", [P, 3])
        rw = take("rw", [P, KD, 36])
        rb = take("rb", [1, 36])
        zero = take("zero", [P, 3 * MAX_ROUNDS * SLOTS * EXPERTS // P])

        x_sb = take("x_sb", [P, TILES, D])
        xnT = take("xnT", [P, KD, PADDED])
        hT_hi = take("hT_hi", [P, KD, PADDED], F32R)
        hT_lo = take("hT_lo", [P, KD, PADDED], F32R)
        oT_hi = take("oT_hi", [P, KD, TOK], F32R)
        oT_lo = take("oT_lo", [P, KD, TOK], F32R)
        hT_at = cursor[0] - 4 * (2 * KD * PADDED + 2 * KD * TOK)
        raw_at = cursor[0]
        raw = [take(f"raw{j}", [P, KD, UNIT]) for j in range(2)]
        split_at = cursor[0]
        w_hi = [take(f"w_hi{j}", [P, KD, UNIT], F32R) for j in range(2)]
        w_lo = [take(f"w_lo{j}", [P, KD, UNIT], F32R) for j in range(2)]
        attn_at = cursor[0]

        stage = [take(f"stage{j}", [P, TILES, UNIT]) for j in range(2)]
        a_kc = [take(f"a_kc{j}", [P, 2, P]) for j in range(2)]
        a_vc = [take(f"a_vc{j}", [P, 2, P]) for j in range(2)]
        qkT = take("qkT", [P, 1024])
        sq = take("sq", [P, TILES, 256])
        ss = take("ss", [P, 12])
        ss_ln = take("ss_ln", [P, 12])
        rs = take("rs", [P, 12])
        rope_x = take("rope_x", [P, TILES, 4, 16])
        rope_y = take("rope_y", [P, TILES, 4, 16])
        probs = [take(f"probs{m}", [P, 704]) for m in range(2)]
        amap = take("amap", [P, 768])
        aT = take("aT", [P, 768])
        v_keep = [take(f"v_keep{j}", [P, TILES, P]) for j in range(2)]
        a_mx = take("a_mx", [P, 2, 3])
        a_nmx = take("a_nmx", [P, 2, 3])
        a_sum = take("a_sum", [P, 2, 3])
        a_rec = take("a_rec", [P, 2, 3])
        osq = take("osq", [P, TILES, P])
        o_ss = take("o_ss", [P, 3])
        o_ln = take("o_ln", [P, 3])
        o_rs = take("o_rs", [P, 3])
        o_n = take("o_n", [P, TILES, P])
        a_end = cursor[0]

        ada_buf = [place(f"ada_buf{n}", [P, KD, ADA_COLS], F32, hT_at + 4 * KD * ADA_COLS * n) for n in range(4)]
        assert hT_at + 16 * KD * ADA_COLS <= raw_at
        first_rows = place("first_rows", [P, 2, ADA_COLS], F32, hT_at + 16 * KD * ADA_COLS)
        assert hT_at + 16 * KD * ADA_COLS + 8 * ADA_COLS <= raw_at
        late_rows = place("late_rows", [P, D], F32, hT_at - 4 * KD * PADDED)
        ada_late = [take(f"ada_late{n}", [P, KD, ADA_COLS]) for n in range(2)]
        cursor[0] = a_end

        xn = place("xn", [P, TILES, D], F32, attn_at)

        cursor[0] = attn_at
        b_qT = [take(f"b_qT{j}", [P, TOK]) for j in range(2)]
        b_kT = [take(f"b_kT{j}", [P, 640]) for j in range(2)]
        b_vT = take("b_vT", [P, PADDED])
        b_v = [take(f"b_v{j}", [P, TILES, P]) for j in range(2)]
        b_ktok = [take(f"b_ktok{j}", [P, TILES, P]) for j in range(2)]
        b_kc = [take(f"b_kc{j}", [P, 2, P]) for j in range(2)]
        b_vc = [take(f"b_vc{j}", [P, 2, P]) for j in range(2)]
        z_na = [take(f"z_na{f}", [P, 2, n]) for f, n in ((0, 384), (1, 192))]
        z_sp = [take(f"z_sp{f}", [P, 2, n]) for f, n in ((0, 384), (1, 192))]
        z_w = [take(f"z_w{f}", [P, 2, n]) for f, n in ((0, 384), (1, 192))]
        b_end = cursor[0]

        sig = [place(f"sig{m}", [P, TOK], F32, attn_at + 4 * TOK * m) for m in range(2)]
        sig_r = [place(f"sig_r{m}", [P, TOK], F32, attn_at + 4 * TOK * (2 + m)) for m in range(2)]
        late = attn_at + 16 * TOK
        g1b = place("g1b", [P, 2, D], F32, late)
        wtmp = place("wtmp", [P, TILES, MIX_COLS], F32, late + 8192)
        cursor[0] = raw_at
        ew = []
        for q in range(4):
            ew.append((take(f"e{q}_w1", [P, KD, FE]), take(f"e{q}_w3", [P, KD, FE]), take(f"e{q}_w2", [P, 2, D])))
        cursor[0] = max(cursor[0], late + 8192 + 4 * TILES * MIX_COLS)
        moe_at = cursor[0]
        g2b = take("g2b", [P, 2, D])
        cursor[0] = hT_at
        h2tok = take("h2tok", [P, TILES, D])
        xn2 = place("xn2", [P, TILES, D], F32, cursor[0])
        ya = take("ya", [P, TILES, D])
        yb = h2tok
        xg = [take(f"xg{q}", [SLOTS, D]) for q in range(4)]
        assert cursor[0] <= raw_at
        cursor[0] = moe_at + 8192
        y_sb = [take(f"y_sb{j}", [SLOTS, D]) for j in range(2)]
        xgT = [take(f"xgT{j}", [P, KD, SLOTS]) for j in range(2)]
        hid = [take(f"hid{j}", [P, 2, SLOTS]) for j in range(2)]
        h_e = [take(f"h_e{j}", [P, 2 * SLOTS]) for j in range(2)]
        h_s = [take(f"h_s{j}", [P, 2 * SLOTS]) for j in range(2)]
        lg = take("lg", [P, TILES, 36])
        gmax = take("gmax", [P, TILES])
        lsub = take("lsub", [P, TILES, 4])
        pgsum = take("pgsum", [P, TILES])
        pg = take("pg", [P, TILES])
        g1h = take("g1h", [P, TILES, 4])
        gtie = take("gtie", [P, TILES, 4])
        gtm = take("gtm", [P, TILES])
        lsel4 = take("lsel4", [P, TILES, 4, 8])
        lsel = take("lsel", [P, TILES, 8])
        etie = take("etie", [P, TILES, 8])
        etm = take("etm", [P, TILES])
        m1 = take("m1", [P, TILES])
        m2 = take("m2", [P, TILES])
        eh1 = take("eh1", [P, TILES, 8])
        eh2 = take("eh2", [P, TILES, 8])
        e2 = take("e2", [P, TILES])
        wsum = take("wsum", [P, TILES])
        pair = [take(f"pair{j}", [P, TILES, 3]) for j in range(2)]
        E1 = [take(f"E{j}", [P, TILES, EXPERTS]) for j in range(2)]
        M = take("M", [P, TILES, EXPERTS])
        rank = take("rank", [P, TILES, EXPERTS])
        rtmp = take("rtmp", [P, TILES, EXPERTS])
        posf = take("posf", [P, 2, TILES])
        posi = take("posi", [P, 2, TILES], U32)
        cnt = take("cnt", [P, 1])
        thr = take("thr", [P, MAX_ROUNDS])
        rnd = take("rnd", [P, 1])
        rnd_i = take("rnd_i", [P, 1], I32)
        tab = take("tab", [SLOTS, EXPERTS, 3])
        tab_i = take("tab_i", [SLOTS, EXPERTS, 2], U32)
        idx = [take(f"idx{q}", [SLOTS, 1], U32) for q in range(4)]
        row_idx = [take(f"row_idx{j}", [SLOTS, 1], U32) for j in range(2)]
        assert cursor[0] <= end, (cursor[0], end)

        ps = ctx.enter_context(nc.psum_tensor("ps", [P, 8, 512], F32))
        h2_dram = nc.dram_tensor("h2_rows", [PADDED, D], F32).ap()
        tab_dram = nc.dram_tensor("slot_table", [MAX_ROUNDS * SLOTS * EXPERTS, 3], F32).ap()
        y_dram = nc.dram_tensor("expert_rows", [1 + 2 * TOK, D], F32).ap()

        small_in = sem("small_in"); rows_in = sem("rows_in"); x_in = sem("x_in"); router_in = sem("router_in")
        setup_done = sem("setup_done"); zero_ready = sem("zero_ready")
        c_act = sem("c_act"); c_dve = sem("c_dve"); vecT_done = sem("vecT_done"); vec_ready = sem("vec_ready")
        raw_loaded = [sem(f"raw_loaded{j}") for j in range(2)]
        ada_in = [sem(f"ada_in{n}") for n in range(4)]; late_in = [sem(f"late_in{n}") for n in range(2)]
        ada_used = sem("ada_used"); late_used = sem("late_used")
        first_out = sem("first_out"); late_out = sem("late_out"); mod_T = sem("mod_T"); mod_ready = sem("mod_ready")
        lam_dve = sem("lam_dve"); lam_act = sem("lam_act")
        n_rstd = sem("n_rstd"); n_scaled = sem("n_scaled"); n_T = sem("n_T")
        n_out_a = sem("n_out_a"); n_out_v = sem("n_out_v")
        h_full = sem("h_full"); h_hi = sem("h_hi"); h_ready = sem("h_ready")
        split_hi = sem("split_hi"); split_done = sem("split_done");
        a_cache = [sem(f"a_cache{j}") for j in range(2)]
        a_proj = sem("a_proj"); a_staged = sem("a_staged")
        a_sq = sem("a_sq"); a_ss = sem("a_ss"); a_rs = sem("a_rs"); a_scaled = sem("a_scaled"); a_roped = sem("a_roped")
        a_stored = [sem(f"a_stored{j}") for j in range(2)]
        a_qkT = sem("a_qkT"); a_qkT_act = sem("a_qkT_act"); a_qkT_dve = sem("a_qkT_dve")
        a_s = [sem(f"a_s{f}") for f in range(2)]
        a_max = [sem(f"a_max{f}") for f in range(2)]
        a_exp = [sem(f"a_exp{f}") for f in range(2)]
        a_comb = sem("a_comb")
        a_aT = sem("a_aT"); a_aT_act = sem("a_aT_act"); a_aT_dve = sem("a_aT_dve")
        a_vkept = sem("a_vkept"); a_pv = sem("a_pv"); a_osq = sem("a_osq"); a_oss = sem("a_oss"); a_ors = sem("a_ors"); a_on = sem("a_on")
        a_oT = sem("a_oT"); a_ohi = sem("a_ohi"); a_olo = sem("a_olo")
        b_cache = [sem(f"b_cache{j}") for j in range(2)]
        b_q = sem("b_q"); b_k = sem("b_k"); b_vp = sem("b_vp")
        b_q_out = sem("b_q_out"); b_k_out = sem("b_k_out"); b_v_out = sem("b_v_out"); b_vT_out = sem("b_vT_out"); b_tv = sem("b_tv")
        b_tk = sem("b_tk"); b_tk_out = sem("b_tk_out"); b_tc = sem("b_tc"); b_tc_out = sem("b_tc_out")
        b_stored = [sem(f"b_stored{j}") for j in range(2)]
        b_z = sem("b_z"); b_zero = sem("b_zero"); b_l = sem("b_l"); b_sp = sem("b_sp"); b_spm = sem("b_spm")
        b_c = sem("b_c"); b_w = sem("b_w"); b_wm = sem("b_wm"); b_o = sem("b_o"); b_ohi = sem("b_ohi"); b_olo = sem("b_olo")
        x_g = sem("x_g"); x_o = sem("x_o"); x_e = sem("x_e"); x_mix = sem("x_mix")
        m_hi = sem("m_hi"); m_ready = sem("m_ready")
        gb_done = sem("gb_done"); gb_ready = sem("gb_ready")
        o_done = sem("o_done"); o_added = sem("o_added")
        h2_ready = sem("h2_ready"); r_T = sem("r_T"); r_rows = sem("r_rows"); 
        r_log = sem("r_log"); r_sub = sem("r_sub"); r_exp = sem("r_exp"); r_e2 = sem("r_e2"); r_e2x = sem("r_e2x")
        r_M = sem("r_M"); r_rank = sem("r_rank"); r_pos = sem("r_pos"); rounds_ready = sem("rounds_ready")
        tab_zero = sem("tab_zero"); tab_put = sem("tab_put"); tab_in = sem("tab_in"); tab_ready = sem("tab_ready")
        idx_ready = [sem(f"idx_ready{j}") for j in range(2)]; row_ready = [sem(f"row_ready{j}") for j in range(2)]
        ew_loaded = [sem(f"ew_loaded{q}") for q in range(4)]
        gathered = [sem(f"gathered{q}") for q in range(4)]
        e_T = [sem(f"e_T{j}") for j in range(2)]
        e_xT = sem("e_xT"); e_exp = sem("e_exp")
        e_h = [sem(f"e_h{j}") for j in range(2)]
        e_hid = [sem(f"e_hid{j}") for j in range(2)]
        e_y = [sem(f"e_y{j}") for j in range(2)]
        e_out_a = [sem(f"e_out_a{j}") for j in range(2)]
        e_out_v = [sem(f"e_out_v{j}") for j in range(2)]
        y_stored = [sem(f"y_stored{j}") for j in range(2)]
        back = sem("back"); y_done = sem("y_done"); stored = sem("stored")

        S_A, S_MIXA, S_B, S_MIXB, S_OUT = 0, 8, 16, 24, 32
        UNITS = S_OUT + 4

        w_in3 = g["w_in"].rearrange("(k p) n -> p k n", p=P)
        w_ada3 = g["w_ada"].rearrange("(k p) n -> p k n", p=P)
        prj3 = [g[n].rearrange("(k p) n -> p k n", p=P) for n in ("w_oa", "w_ob", "w_out")]

        def f32(ap):
            return ap.bitcast(F32)

        def at(r, i, u):
            return u % 4, u % 2, 8 * r + i + u // 4, 16 * r + 2 * i + u // 2, 32 * r + 4 * i + u, 4 * i + u

        block = ctx.enter_context(nc.Block())

        @block.sync
        def _(sp):
            sp.dma_start(cst[:], g["shape_constants"]).then_inc(small_in, 16)
            sp.dma_start(vec_rows[64:72, :], g["c_prompt"].rearrange("a (k p) -> (a k) p", p=P)).then_inc(small_in, 16)
            sp.dma_start(vec_rows[72:80, :], g["c_sample"].rearrange("a (k p) -> (a k) p", p=P)).then_inc(small_in, 16)
            sp.dma_start(vec_rows[0:48, :], g["b_ada"].rearrange("(k p) -> k p", p=P)).then_inc(small_in, 16)
            sp.dma_start(vec_rows[48:56, :], g["norm1_g"].rearrange("(k p) -> k p", p=P)).then_inc(small_in, 16)
            sp.dma_start(vec_rows[56:64, :], g["norm2_g"].rearrange("(k p) -> k p", p=P)).then_inc(small_in, 16)

            def load_unit(base, h, j):
                for n in range(3):
                    sp.dma_start(raw[j][:, :, n * P:(n + 1) * P],
                                 w_in3[:, :, bass.ds(base + n * D + h * P, P)]).then_inc(raw_loaded[j], 16)

            def load_ada(c):
                sp.dma_start(ada_buf[c % 4][:], w_ada3[:, :, c * ADA_COLS:(c + 1) * ADA_COLS]).then_inc(ada_in[c % 4], 16)

            def load_late(h, n):
                if not (isinstance(h, int) and h == 0):
                    sp.wait_ge(late_used, 2 * h + n - 1)
                sp.dma_start(ada_late[n][:], w_ada3[:, :, bass.ds((8 + 2 * h + n) * ADA_COLS, ADA_COLS)]).then_inc(late_in[n], 16)

            load_ada(0)
            load_ada(1)
            sp.dma_start(x_sb[:, 0:2, :], g["x_prompt"][0].rearrange("(t p) d -> p t d", p=P)).then_inc(x_in, 16)
            sp.dma_start(x_sb[0:DEC, 2, :], g["x_sample"][0]).then_inc(x_in, 16)
            for n, name in enumerate(("a_lam_q1", "a_lam_k1", "a_lam_q2", "a_lam_k2")):
                sp.dma_start(lam_rows[:, n, :], g[name].partition_broadcast(P)).then_inc(rows_in, 16)
            for n in range(4):
                sp.dma_start(gqk[:, n, :], g["a_qnorm_g" if n < 2 else "a_knorm_g"].partition_broadcast(P)).then_inc(rows_in, 16)
            sp.dma_start(subln[:], g["a_subln_g"].rearrange("(p a) -> p a", a=1)).then_inc(rows_in, 16)
            sp.dma_start(rw[:, :, 0:4], g["w_rg"].rearrange("(k p) n -> p k n", p=P)).then_inc(router_in, 16)
            sp.dma_start(rw[:, :, 4:36], g["w_re"].rearrange("(k p) n -> p k n", p=P)).then_inc(router_in, 16)
            sp.dma_start(rb[:, 0:4], g["b_rg"].rearrange("(a n) -> a n", a=1)).then_inc(router_in, 16)
            sp.dma_start(rb[:, 4:36], g["b_re"].rearrange("(a n) -> a n", a=1)).then_inc(router_in, 16)
            sp.wait_ge(zero_ready, 1)
            sp.dma_start(tab_dram.rearrange("(p n) a -> p (n a)", p=P), zero[:]).then_inc(tab_zero, 16)
            load_ada(2)
            load_ada(3)
            load_unit(0, 0, 0)
            for c in range(4, 8):
                sp.wait_ge(ada_used, c - 3)
                load_ada(c)
            load_unit(0, 1, 1)

            def load_prj(j, src, c):
                sp.dma_start(raw[j][:, :, 0:MIX_COLS], src[:, :, bass.ds(c * MIX_COLS, MIX_COLS)]).then_inc(raw_loaded[j], 48)

            def cache(kc, vc, ks, vs, h, s):
                sp.dma_start(kc[:], ks.rearrange("(t p) n -> p t n", p=P)[:, :, bass.ds(h * P, P)]).then_inc(s, 16)
                sp.dma_start(vc[:], vs.rearrange("(t p) n -> p t n", p=P)[:, :, bass.ds(h * P, P)]).then_inc(s, 16)

            def store(src_k, src_v, outs, h, s):
                kp, vp, kss, vss = outs
                for dst, src in ((kp, src_k), (vp, src_v)):
                    sp.dma_start(dst.rearrange("(t p) n -> p t n", p=P)[:, :, bass.ds(h * P, P)], src[:, 0:2, :]).then_inc(s, 16)
                for dst, src in ((kss, src_k), (vss, src_v)):
                    sp.dma_start(dst[:, bass.ds(h * P, P)], src[0:DEC, 2, :]).then_inc(s, 16)

            def a_cache_load(h, j, first):
                if not first:
                    sp.wait_ge(a_qkT, h - 1)
                    sp.wait_ge(a_pv, h - 1)
                cache(a_kc[j], a_vc[j], g["cache_a_k"], g["cache_a_v"], h, a_cache[j])

            def a_weights(h, j):
                sp.wait_ge(split_done, S_A + h + 1)
                load_unit(0, h + 2, j)

            def a_store(h, j):
                sp.wait_ge(a_roped, h + 1)
                store(stage[j][:, :, P:2 * P], stage[j][:, :, 2 * P:3 * P],
                      [t_out[n] for n in ("a_k_prompt", "a_v_prompt", "a_k_sample", "a_v_sample")], h, a_stored[j])

            sp.wait_ge(n_T, KD)
            a_cache_load(0, 0, True)
            a_cache_load(1, 1, True)
            a_weights(0, 0)
            a_weights(1, 1)
            a_store(0, 0)
            for n in range(2):
                load_late(0, n)
            with sp.Fori(1, 3) as i:
                for j in range(2):
                    a_weights(2 * i + j, j)
                    a_store(2 * i + j - 1, 1 - j)
                    a_cache_load(2 * i + j, j, False)
                    for n in range(2):
                        load_late(2 * i + j - 1, n)
            for j in range(2):
                sp.wait_ge(split_done, S_A + 7 + j)
                load_prj(j, prj3[0] if j else w_in3[:, :, 6 * D:7 * D], 0)
                a_store(5 + j, 1 - j)
                a_cache_load(6 + j, j, False)
                for n in range(2):
                    load_late(5 + j, n)
            a_store(7, 1)
            for n in range(2):
                load_late(7, n)

            def mix_loads(gate_col, prj, s0, c):
                for j in range(2):
                    units = sp.to_reg(s0 + 2 * c - 1 + j)
                    sp.wait_ge(small_in, 16)
                    sp.wait_ge(split_done, units)
                    load_prj(j, prj if j else w_in3[:, :, gate_col:gate_col + D], c)

            with sp.Fori(1, 4) as c:
                mix_loads(6 * D, prj3[0], S_MIXA, c)
            for j in range(2):
                sp.wait_ge(split_done, S_B - 1 + j)
                load_unit(3 * D, j, j)

            def b_iteration(p, j, load, first):
                if load:
                    sp.wait_ge(split_done, S_B + p + 1)
                    load_unit(3 * D, p + 2, j)
                if first:
                    sp.wait_ge(a_olo, A_HEADS)
                    sp.wait_ge(x_mix, 8)
                    sp.wait_ge(a_stored[j], 4 * 64)
                    sp.wait_ge(a_stored[1 - j], 4 * 64)
                else:
                    sp.wait_ge(b_tc, p - 1)
                    sp.wait_ge(b_o, p - 1)
                cache(b_kc[j], b_vc[j], g["cache_b_k"], g["cache_b_v"], p, b_cache[j])

            def b_store(p, j):
                sp.wait_ge(b_tk_out, p + 1)
                sp.wait_ge(b_v_out, p + 1)
                store(b_ktok[j][:], b_v[j][:],
                      [t_out[n] for n in ("b_k_prompt", "b_v_prompt", "b_k_sample", "b_v_sample")], p, b_stored[j])

            b_iteration(0, 0, True, True)
            b_iteration(1, 1, True, True)
            b_store(0, 0)
            with sp.Fori(1, 3) as i:
                for j in range(2):
                    b_iteration(2 * i + j, j, True, False)
                    b_store(2 * i + j - 1, 1 - j)
            for j in range(2):
                b_iteration(6 + j, j, False, False)
                sp.wait_ge(split_done, S_B + 7 + j)
                load_prj(j, prj3[1] if j else w_in3[:, :, 7 * D:8 * D], 0)
                b_store(5 + j, 1 - j)
            b_store(7, 1)
            with sp.Fori(1, 4) as c:
                mix_loads(7 * D, prj3[1], S_MIXB, c)
            for u in range(4):
                sp.wait_ge(split_done, S_OUT - 1 + u)
                load_prj(u % 2, prj3[2], u)

            def load_expert(q, e):
                w1s, w3s, w2s = ew[q]
                sp.dma_start(w1s[:], g["w1"].rearrange("e (p k) f -> e p k f", k=KD)[e]).then_inc(ew_loaded[q], 16)
                sp.dma_start(w3s[:], g["w3"].rearrange("e (p k) f -> e p k f", k=KD)[e]).then_inc(ew_loaded[q], 16)
                sp.dma_start(w2s[:], g["w2"].rearrange("e (p m) d -> e p m d", m=2)[e]).then_inc(ew_loaded[q], 16)

            sp.wait_ge(split_done, S_OUT + 4)
            sp.wait_ge(o_done, 12)
            sp.wait_ge(o_added, 12)
            count = sp.alloc_register("sp_rounds")
            sp.reg_mov(count, 1)
            with sp.Fori(0, count) as r:
                with sp.Fori(0, 8) as i:
                    for q in range(4):
                        sp.wait_ge(e_y[q % 2], 16 * r + 2 * i + q // 2 + 1)
                        load_expert(q, 4 * i + q)
                sp.wait_ge(rounds_ready, 1)
                sp.reg_load(count, rnd_i[0:1, 0:1])
            sp.wait_ge(y_done, 2)
            sp.dma_start(t_out["y_prompt"].rearrange("(t p) d -> p t d", p=P), x_sb[:, 0:2, :]).then_inc(stored, 16)
            sp.dma_start(t_out["y_sample"], x_sb[0:DEC, 2, :]).then_inc(stored, 16)
            sp.wait_ge(stored, 32)
            for s in a_stored + b_stored:
                sp.wait_ge(s, 4 * 64)

        @block.tensor
        def _(pe):
            def bank(b):
                return ps[:, b, :]

            def mm3(out, lhs_hi, lhs_lo, rhs_hi, rhs_lo, first, last):
                nc.tensor.matmul(out, lhs_hi, rhs_hi, start=first, stop=False, skip_group_check=True)
                nc.tensor.matmul(out, lhs_hi, rhs_lo, start=False, stop=False, skip_group_check=True)
                return nc.tensor.matmul(out, lhs_lo, rhs_hi, start=False, stop=last, skip_group_check=True)

            def mm(out, lhs, rhs, first, last=True):
                return nc.tensor.matmul(out, lhs, rhs, start=first, stop=last, skip_group_check=True)

            for s in e_T + e_h + e_y + e_y:
                pe.nop().then_inc(s, 1)
            pe.wait_ge(c_dve, 1)
            nc.tensor.transpose(ps[:, 0, 0:80], vec_rows[:], ident[0:80, 0:80]).then_inc(vecT_done, 1)
            pe.wait_ge(vec_ready, 1)

            def ada(buf, out, done):
                for m in range(len(out)):
                    n = ADA_COLS // len(out)
                    for k in range(KD):
                        last = mm(out[m], c_cols[:, k, :], buf[:, k, m * n:(m + 1) * n], k == 0, k == KD - 1)
                last.then_inc(done, 1)

            def rows_to_columns(src, k, b):
                for t in range(TILES):
                    last = nc.tensor.transpose(ps[:, b, t * P:(t + 1) * P], src[:, t, k * P:(k + 1) * P], ident)
                return last

            def first_chunks(i):
                for j in range(4):
                    pe.wait_ge(ada_in[j], 16 * (i + 1))
                    ada(ada_buf[j], [ps[32 * j:32 * j + 32, 7, i * ADA_COLS:(i + 1) * ADA_COLS]], ada_used)

            first_chunks(0)
            pe.wait_ge(n_scaled, 3)
            for k in range(KD - 1):
                rows_to_columns(xn, k, k).then_inc(n_T, 1)
            pe.wait_ge(n_out_a, 1)
            rows_to_columns(xn, KD - 1, 0).then_inc(n_T, 1)
            pe.wait_ge(first_out, 1)
            first_chunks(1)
            pe.wait_ge(first_out, 2)
            pe.wait_ge(n_out_v, 3)
            for n in range(4):
                last = nc.tensor.transpose(ps[:, 5, n * P:(n + 1) * P], first_rows[:, n // 2, (n % 2) * P:(n % 2 + 1) * P], ident)
            last.then_inc(mod_T, 1)

            def ada_chunk(h, n):
                pe.wait_ge(late_in[n], 16 * (h - 2))
                ada(ada_late[n], [ps[32 * b:32 * b + 32, 7, 384:512] for b in (2 * n, 2 * n + 1)], late_used)

            pe.wait_ge(h_ready, 2)

            def mix_part(c, s0, j, first):
                rhs_hi, rhs_lo, done, used = ((hT_hi, hT_lo, x_g, x_e), (oT_hi, oT_lo, x_o, x_mix))[j]
                pe.wait_ge(split_done, s0 + 2 * c + j + 1)
                if not first:
                    pe.wait_ge(used, (0 if s0 == S_MIXA else 8) + 2 * c)
                for m in range(2):
                    sl = slice(m * P, (m + 1) * P)
                    for k in range(KD):
                        last = mm3(ps[:, 2 * j + m, 0:TOK], w_hi[j][:, k, sl], w_lo[j][:, k, sl],
                                   rhs_hi[:, k, 0:TOK], rhs_lo[:, k, 0:TOK], k == 0, k == KD - 1)
                last.then_inc(done, 1)

            def gate(c, s0, first):
                mix_part(c, s0, 0, first)

            def mix(c, s0, first):
                if not first:
                    gate(c, s0, False)
                mix_part(c, s0, 1, first)

            def proj_tile(h, j, t, first):
                if t == 0:
                    pe.wait_ge(split_done, S_A + h + 1)
                if not first:
                    pe.wait_ge(a_staged, 3 * h - 2 + t)
                for k in range(KD):
                    sl = slice(t * P, (t + 1) * P)
                    last = mm3(ps[:, t, 0:UNIT], hT_hi[:, k, sl], hT_lo[:, k, sl], w_hi[j][:, k, :], w_lo[j][:, k, :],
                               k == 0, k == KD - 1)
                last.then_inc(a_proj, 1)

            def a_iteration(h, j, P_on, qk_on, s1_on, o_on, cache_value):
                jq = 1 - j
                if P_on:
                    proj_tile(h, j, 0, isinstance(h, int) and h == 0)
                if o_on:
                    l = h - 3
                    pe.wait_ge(a_aT_act, l + 1)
                    pe.wait_ge(a_aT_dve, l + 1)
                    pe.wait_ge(a_vkept, l + 1)
                    pe.wait_ge(a_on, l)
                    if not (isinstance(h, int) and h == 3):
                        pe.wait_ge(late_out, l)
                    v, vc = v_keep[jq], a_vc[jq]
                    for t, pairs in ((0, ((0, v[:, 0, :]),)), (1, ((1, v[:, 0, :]), (2, v[:, 1, :]))),
                                     (2, ((3, vc[:, 0, :]), (4, vc[:, 1, :]), (5, v[:, 2, :])))):
                        for n, (blk, rhs) in enumerate(pairs):
                            last = mm(ps[:, 7, t * P:(t + 1) * P], aT[:, blk * P:(blk + 1) * P], rhs,
                                      n == 0, n == len(pairs) - 1)
                    last.then_inc(a_pv, 1)
                if s1_on:
                    pe.wait_ge(a_exp[0], h - 1)
                    for mp in range(2):
                        r = slice(64 * mp, 64 * mp + 64)
                        last = mm(ps[:, 5 + mp, 0:320], qkT[r, 256:384], qkT[r, 640:960], True)
                    last.then_inc(a_s[1], 1)
                if P_on:
                    proj_tile(h, j, 1, isinstance(h, int) and h == 0)
                if isinstance(h, int) and h == 8:
                    pe.wait_ge(a_staged, 24)
                    gate(0, S_MIXA, True)
                if o_on:
                    l = h - 3
                    pe.wait_ge(a_on, l + 1)
                    for t in range(TILES):
                        last = nc.tensor.transpose(ps[:, 4, t * P:(t + 1) * P], o_n[:, t, :], ident)
                    last.then_inc(a_oT, 1)
                    ada_chunk(h, 0)
                if qk_on:
                    m = h - 1
                    pe.wait_ge(a_roped, m + 1)
                    pe.wait_ge(a_cache[jq], cache_value)
                    st = stage[jq]
                    for n, src in enumerate((st[:, 0, 0:P], st[:, 1, 0:P], st[:, 2, 0:P], st[:, 0, P:2 * P])):
                        nc.tensor.transpose(ps[:, 3, n * P:(n + 1) * P], src, ident)
                    if o_on:
                        ada_chunk(h, 1)
                        pe.wait_ge(a_olo, h - 2)
                    for n, src in enumerate((st[:, 1, P:2 * P], a_kc[jq][:, 0, :], a_kc[jq][:, 1, :], st[:, 2, P:2 * P])):
                        last = nc.tensor.transpose(ps[:, 4, n * P:(n + 1) * P], src, ident)
                    last.then_inc(a_qkT, 1)
                elif o_on:
                    ada_chunk(h, 1)
                if P_on:
                    proj_tile(h, j, 2, isinstance(h, int) and h == 0)
                if s1_on:
                    pe.wait_ge(a_comb, 2 * h - 2)
                    if qk_on:
                        pe.wait_ge(a_qkT_act, h)
                        pe.wait_ge(a_qkT_dve, h)
                    elif o_on:
                        pe.wait_ge(a_olo, h - 2)
                    for n in range(6):
                        b, c = (3, n) if n < 4 else (4, n - 4)
                        last = nc.tensor.transpose(ps[:, b, c * P:(c + 1) * P], amap[:, n * P:(n + 1) * P], ident)
                    last.then_inc(a_aT, 1)
                if qk_on:
                    pe.wait_ge(a_qkT_act, h)
                    pe.wait_ge(a_qkT_dve, h)
                    if s1_on:
                        pe.wait_ge(a_exp[1], h - 1)
                    for mp in range(2):
                        r = slice(64 * mp, 64 * mp + 64)
                        mm(ps[:, 5 + mp, 0:128], qkT[r, 0:128], qkT[r, 384:512], True)
                        last = mm(ps[:, 5 + mp, 128:384], qkT[r, 128:256], qkT[r, 384:640], False)
                    last.then_inc(a_s[0], 1)

            for h in range(4):
                a_iteration(h, h % 2, True, h >= 1, h >= 2, h >= 3, 32 * ((h - 1) // 2 + 1))
            with pe.Fori(2, 4) as i:
                for j in range(2):
                    a_iteration(2 * i + j, j, True, True, True, True, 32 * (i + j))
            for h in range(8, 11):
                a_iteration(h, h % 2, False, h < 9, h < 10, True, 128)
            pe.wait_ge(late_out, 8)
            for n in range(8):
                last = nc.tensor.transpose(ps[:, 5 + n // 4, (n % 4) * P:(n % 4 + 1) * P], late_rows[:, n * P:(n + 1) * P], ident)
            last.then_inc(mod_T, 1)

            pe.wait_ge(a_olo, 8)
            mix(0, S_MIXA, True)
            with pe.Fori(1, 4) as c:
                mix(c, S_MIXA, False)

            def b_iteration(p, j, P_on, z_on, w_on, first, cache_value):
                jz = 1 - j
                if P_on:
                    pe.wait_ge(split_done, S_B + p + 1)
                    if first:
                        pe.wait_ge(x_e, 8)
                        pe.wait_ge(x_mix, 8)
                    else:
                        pe.wait_ge(b_vT_out, p)
                    for k in range(KD):
                        last = mm3(ps[:, 0, 0:TOK], w_hi[j][:, k, 0:P], w_lo[j][:, k, 0:P],
                                   hT_hi[:, k, 0:TOK], hT_lo[:, k, 0:TOK], k == 0, k == KD - 1)
                    last.then_inc(b_q, 1)
                if w_on:
                    l = p - 2
                    pe.wait_ge(b_wm, l + 1)
                    if not (isinstance(p, int) and p == 2):
                        pe.wait_ge(b_olo, l)
                    pe.wait_ge(b_v_out, l + 1)
                    v, vc = b_v[j], b_vc[j]
                    for hh in range(2):
                        c = slice(64 * hh, 64 * hh + 64)
                        o = ps[c, 3, :]
                        mm(o[:, 0:256], v[:, 0, c], z_w[0][:, hh, 0:256], True)
                        mm(o[:, 128:256], v[:, 1, c], z_w[0][:, hh, 256:384], False)
                        mm(o[:, 256:320], vc[:, 0, c], z_w[1][:, hh, 0:64], False)
                        mm(o[:, 256:320], vc[:, 1, c], z_w[1][:, hh, 64:128], False)
                        last = mm(o[:, 256:320], v[:, 2, c], z_w[1][:, hh, 128:192], False)
                    last.then_inc(b_o, 1)
                if z_on:
                    pe.wait_ge(b_q_out, p)
                    pe.wait_ge(b_k_out, p)
                    pe.wait_ge(b_tc_out, p)
                    if isinstance(p, int) and p == 1:
                        pe.wait_ge(b_zero, 1)
                    if w_on:
                        pe.wait_ge(b_w, p - 1)
                    kT, qT = b_kT[jz], b_qT[jz]
                    for hh in range(2):
                        r = slice(64 * hh, 64 * hh + 64)
                        zp, zs = ps[:, 4 + hh, :], ps[:, 6 + hh, :]
                        mm(zp[:, 0:256], kT[r, 0:128], qT[r, 0:256], True)
                        mm(zp[:, 256:384], kT[r, 128:256], qT[r, 128:256], False)
                        mm(zs[:, 0:64], kT[r, 384:512], qT[r, 256:320], True)
                        mm(zs[:, 64:128], kT[r, 512:640], qT[r, 256:320], False)
                        last = mm(zs[:, 128:192], kT[r, 256:384], qT[r, 256:320], False)
                    last.then_inc(b_z, 1)
                if P_on:
                    if not first:
                        pe.wait_ge(b_k_out, p)
                    for k in range(KD):
                        last = mm3(ps[:, 1, 0:TOK], w_hi[j][:, k, P:2 * P], w_lo[j][:, k, P:2 * P],
                                   hT_hi[:, k, 0:TOK], hT_lo[:, k, 0:TOK], k == 0, k == KD - 1)
                    last.then_inc(b_k, 1)
                if z_on:
                    for t in range(TILES):
                        last = nc.tensor.transpose(ps[:, 2, t * P:(t + 1) * P], b_kT[jz][:, t * P:(t + 1) * P], ident)
                    last.then_inc(b_tk, 1)
                    pe.wait_ge(b_vT_out, p)
                    if w_on:
                        pe.wait_ge(b_olo, p - 1)
                    for t in range(TILES):
                        last = nc.tensor.transpose(ps[:, 3, t * P:(t + 1) * P], b_vT[:, t * P:(t + 1) * P], ident)
                    last.then_inc(b_tv, 1)
                    if isinstance(p, int) and p == 8:
                        pe.wait_ge(b_k_out, 8)
                        gate(0, S_MIXB, True)
                if P_on:
                    pe.wait_ge(b_q_out, p + 1)
                    for k in range(KD):
                        last = mm3(ps[:, 0, 0:TOK], w_hi[j][:, k, 2 * P:3 * P], w_lo[j][:, k, 2 * P:3 * P],
                                   hT_hi[:, k, 0:TOK], hT_lo[:, k, 0:TOK], k == 0, k == KD - 1)
                    last.then_inc(b_vp, 1)
                if z_on:
                    pe.wait_ge(b_spm, p)
                    for hh in range(2):
                        zp, zs = ps[:, 4 + hh, :], ps[:, 6 + hh, :]
                        a, s = z_sp[0][:, hh, :], z_sp[1][:, hh, :]
                        mm(zp[:, 0:384], tri_neg, a, False)
                        mm(zp[:, 128:256], ones_neg[:], a[:, 256:384], False)
                        mm(zs[:, 0:192], tri_neg, s, False)
                        mm(zs[:, 0:64], ones_neg[:], s[:, 64:128], False)
                        mm(zs[:, 0:64], ones_neg[:], s[:, 128:192], False)
                        last = mm(zs[:, 64:128], ones_neg[:], s[:, 128:192], False)
                    last.then_inc(b_c, 1)
                if P_on:
                    if z_on:
                        pe.wait_ge(b_tk_out, p)
                    pe.wait_ge(b_cache[j], cache_value)
                    for n in range(2):
                        last = nc.tensor.transpose(ps[:, 2, n * P:(n + 1) * P], b_kc[j][:, n, :], ident)
                    last.then_inc(b_tc, 1)

            b_iteration(0, 0, True, False, False, True, 32)
            b_iteration(1, 1, True, True, False, False, 32)
            with pe.Fori(1, 4) as i:
                for j in range(2):
                    b_iteration(2 * i + j, j, True, True, True, False, 32 * (i + 1))
            b_iteration(8, 0, False, True, True, False, 0)
            b_iteration(9, 1, False, False, True, False, 0)

            pe.wait_ge(mod_ready, 2)
            pe.wait_ge(b_olo, 8)
            pe.wait_ge(b_v_out, 8)
            pe.wait_ge(b_tk_out, 8)
            mix(0, S_MIXB, True)
            with pe.Fori(1, 4) as c:
                mix(c, S_MIXB, False)

            pe.wait_ge(x_mix, 16)
            for n, col in enumerate((16, 40)):
                for s in range(2):
                    if n:
                        pe.wait_ge(gb_ready, s + 1)
                    for k in range(KD):
                        last = mm(ps[:, 4 + 2 * s + k // 4, (k % 4) * P:(k % 4 + 1) * P],
                                  mod[:, col + k, s:s + 1].broadcast_to([P, P]), ident, k % 4 == 0)
                    last.then_inc(gb_done, 1)

            pe.wait_ge(m_ready, 1)
            for u in range(4):
                pe.wait_ge(split_done, S_OUT + u + 1)
                for t in range(TILES):
                    b = t + 3 * (u % 2)
                    if u == 1:
                        pe.wait_ge(gb_ready, 4)
                    elif u > 1:
                        pe.wait_ge(o_added, 3 * (u - 2) + t + 1)
                    for k in range(KD):
                        sl = slice(t * P, min((t + 1) * P, TOK))
                        last = mm3(ps[0:rows_of(t), b, 0:MIX_COLS], oT_hi[:, k, sl], oT_lo[:, k, sl],
                                   w_hi[u % 2][:, k, 0:MIX_COLS], w_lo[u % 2][:, k, 0:MIX_COLS], k == 0, k == KD - 1)
                    last.then_inc(o_done, 1)

            pe.wait_ge(n_scaled, 6)
            pe.wait_ge(gb_ready, 4)
            for k in range(KD - 1):
                rows_to_columns(xn2, k, k).then_inc(n_T, 1)
            pe.wait_ge(n_out_a, 5)
            rows_to_columns(xn2, KD - 1, 0).then_inc(n_T, 1)
            pe.wait_ge(h2_ready, 2)
            pe.wait_ge(router_in, 64)
            for t in range(TILES):
                for k in range(KD):
                    mm(ps[:, 1, t * 36:(t + 1) * 36], xnT[:, k, t * P:(t + 1) * P], rw[:, k, :], k == 0, False)
                last = mm(ps[:, 1, t * 36:(t + 1) * 36], ones[0:1, :], rb[:], False)
            last.then_inc(r_log, 1)
            for t in range(TILES):
                for half in range(2):
                    b = 2 + 2 * t + half if t < 2 else 6 + half
                    for k in range(4):
                        last = nc.tensor.transpose(ps[:, b, k * P:(k + 1) * P], xnT[:, 4 * half + k, t * P:(t + 1) * P], ident)
                    last.then_inc(r_T, 1)
            pe.wait_ge(r_M, 1)
            for t in range(TILES):
                for u in range(t):
                    mm(ps[:, 0, t * EXPERTS:(t + 1) * EXPERTS], ones[:], M[:, u, :], u == 0, False)
                mm(ps[:, 0, t * EXPERTS:(t + 1) * EXPERTS], before, M[:, t, :], t == 0)
            for t in range(TILES):
                last = mm(ps[:, 0, 3 * EXPERTS:4 * EXPERTS], ones[:], M[:, t, :], t == 0, t == 2)
            last.then_inc(r_rank, 1)

            pe.wait_ge(rounds_ready, 1)
            pe.wait_ge(r_rows, 6)
            rounds = pe.value_load(rnd_i[0:1, 0:1], min_val=1, max_val=MAX_ROUNDS)

            def gather_T(x):
                q, j, n4, n2, n, e = x
                rows, copied = pe.to_reg(16 * (n4 + 1)), pe.to_reg(n + 1)
                pe.wait_ge(rounds_ready, 1)
                pe.wait_ge(gathered[q], rows)
                pe.wait_ge(e_xT, copied)
                for k in range(KD):
                    last = nc.tensor.transpose(ps[:, j, k * SLOTS:(k + 1) * SLOTS], xg[q][:, k:D:KD], ident[0:SLOTS, 0:SLOTS])
                last.then_inc(e_T[j], 1)
                pe.free_register(rows)
                pe.free_register(copied)

            def hidden(x):
                q, j, n4, n2, n, e = x
                pe.wait_ge(ew_loaded[q], 48 * (n4 + 1))
                pe.wait_ge(e_xT, n + 3)
                pe.wait_ge(e_hid[j], n2 + 1)
                for w in range(2):
                    for m in range(2):
                        for k in range(KD):
                            c = (2 * w + m) * SLOTS
                            last = mm(ps[:, 2 + j, c:c + SLOTS], ew[q][w][:, k, m:FE:2], xgT[j][:, k, :], k == 0, k == KD - 1)
                last.then_inc(e_h[j], 1)

            def down(x):
                q, j, n4, n2, n, e = x
                pe.wait_ge(e_hid[j], n2 + 2)
                pe.wait_ge(e_out_a[j], n2 + 1)
                pe.wait_ge(e_out_v[j], n2 + 1)
                for half in range(2):
                    for m in range(2):
                        last = mm(ps[0:SLOTS, 4 + 2 * j + half, :], hid[j][:, m, :], ew[q][2][:, m, half * 512:(half + 1) * 512],
                                  m == 0, m == 1)
                last.then_inc(e_y[j], 1)

            with pe.Fori(0, rounds) as r:
                gather_T(at(r, 0, 0))
                gather_T(at(r, 0, 1))
                hidden(at(r, 0, 0))
                with pe.Fori(0, 7) as i:
                    for u in range(1, 5):
                        gather_T(at(r, i, u + 1))
                        hidden(at(r, i, u))
                        down(at(r, i, u - 1))
                for u in range(29, 32):
                    if u < 31:
                        gather_T(at(r, 0, u + 1))
                    hidden(at(r, 0, u))
                    down(at(r, 0, u - 1))
                down(at(r, 0, 31))

        @block.scalar
        def _(act):
            A = nc.scalar.activation
            nc.scalar.preload_act_table_set("natural_log_exp_and_others")
            act.wait_ge(small_in, 96)
            A(c_sig[64:80, :], vec_rows[64:80, :], ACT.Exp, scale=-1.0).then_inc(c_act, 1)

            def root(dst, tmp, src, n, done):
                A(tmp, src, ACT.Ln, bias=eps[:, 0:1], scale=1.0 / n)
                act.drain()
                A(dst, tmp, ACT.Exp, scale=-0.5).then_inc(done, 1)

            def norm_rows(scratch):
                for t in range(TILES):
                    A(scratch[:, t, :], x_sb[:, t, :], ACT.Square, accum_out=stat[:, t:t + 1])
                act.drain()
                root(rstd[:], stat_ln[:], stat[:], D, n_rstd)

            def norm_out(n0):
                for k in range(0, KD, 2):
                    act.wait_ge(n_T, n0 + k + 1)
                    A(xnT[:, k, :], ps[:, k, 0:PADDED], ACT.Copy).then_inc(n_out_a, 1)

            act.wait_ge(setup_done, 1)
            act.wait_ge(x_in, 32)
            norm_rows(xn)
            act.wait_ge(lam_dve, 1)
            A(lam_exp[:], lam_sum[:], ACT.Exp).then_inc(lam_act, 1)

            def modulation_rows(i):
                act.wait_ge(ada_used, 4 * (i + 1))
                A(first_rows[:, i, :], ps[:, 7, i * ADA_COLS:(i + 1) * ADA_COLS], ACT.Copy).then_inc(first_out, 1)

            modulation_rows(0)
            norm_out(0)

            def split(j, loaded, used, width=UNIT):
                act.wait_ge(raw_loaded[j], loaded)
                if used is not None:
                    act.wait_ge(*used)
                A(w_hi[j][:, :, 0:width], raw[j][:, :, 0:width], ACT.Copy).then_inc(split_hi, 1)

            split(0, 48, None)
            modulation_rows(1)
            for n in range(2):
                act.wait_ge(h_full, n + 1)
                A(hT_hi[:, 4 * n:4 * n + 4, :], xnT[:, 4 * n:4 * n + 4, :], ACT.Copy).then_inc(h_hi, 1)

            def a_iteration(h, j, P_on, qk_on, s1_on, o_on, loaded, store_value):
                jq = 1 - j
                if qk_on:
                    act.wait_ge(a_staged, 3 * h)
                    if not (isinstance(h, int) and h == 1):
                        act.wait_ge(a_ss, h - 1)
                    A(sq[:], stage[jq][:, :, 0:256], ACT.Square).then_inc(a_sq, 1)
                    act.wait_ge(a_ss, h)
                    if not (isinstance(h, int) and h == 1):
                        act.wait_ge(a_scaled, h - 1)
                    root(rs[:], ss_ln[:], ss[:], 64, a_rs)
                if loaded is not None:
                    split(jq, loaded, None if isinstance(h, int) and h == 0 else (a_proj, 3 * h),
                          MIX_COLS if isinstance(h, int) and h >= 7 else UNIT)

                def stage_out(t):
                    act.wait_ge(a_proj, 3 * h + t + 1)
                    if t == 0:
                        if store_value is not None:
                            act.wait_ge(a_stored[j], store_value)
                            act.wait_ge(a_qkT, h - 1)
                            act.wait_ge(a_vkept, h - 1)
                    A(stage[j][:, t, :], ps[:, t, 0:UNIT], ACT.Copy).then_inc(a_staged, 1)

                if P_on:
                    stage_out(0)
                if o_on:
                    act.wait_ge(a_pv, h - 2)
                    A(osq[:], ps[:, 7, 0:PADDED].rearrange("p (t c) -> p t c", t=TILES), ACT.Square).then_inc(a_osq, 1)
                    act.wait_ge(a_oss, h - 2)
                    root(o_rs[:], o_ln[:], o_ss[:], P, a_ors)
                if s1_on:
                    act.wait_ge(a_max[1], h - 1)
                    for mp in range(2):
                        last = A(probs[mp][:, 384:704], ps[:, 5 + mp, 0:320], ACT.Exp, bias=a_nmx[:, mp, 2:3],
                                 accum_out=a_sum[:, mp, 2:3])
                    last.then_inc(a_exp[1], 1)
                if P_on:
                    stage_out(1)
                if o_on:
                    act.wait_ge(a_oT, h - 2)
                    A(oT_hi[:, bass.ds(h - 3, 1), :].rearrange("p a n -> p (a n)"), ps[:, 4, 0:TOK], ACT.Copy,
                      scale=subln[:, 0:1]).then_inc(a_ohi, 1)
                if qk_on:
                    act.wait_ge(a_qkT, h)
                    A(qkT[:, 0:512], ps[:, 3, :], ACT.Copy).then_inc(a_qkT_act, 1)
                if o_on:
                    act.wait_ge(late_used, 2 * h - 4)
                    A(late_rows[:, bass.ds((h - 3) * P, P)], ps[:, 7, 384:512], ACT.Copy).then_inc(late_out, 1)
                if P_on:
                    stage_out(2)
                if s1_on:
                    act.wait_ge(a_aT, h - 1)
                    A(aT[:, 0:512], ps[:, 3, :], ACT.Copy).then_inc(a_aT_act, 1)
                if qk_on:
                    act.wait_ge(a_max[0], h)
                    for mp in range(2):
                        for t, sl in ((0, slice(0, 128)), (1, slice(128, 384))):
                            last = A(probs[mp][:, sl], ps[:, 5 + mp, sl], ACT.Exp, bias=a_nmx[:, mp, t:t + 1],
                                     accum_out=a_sum[:, mp, t:t + 1])
                    last.then_inc(a_exp[0], 1)

            for h in range(4):
                a_iteration(h, h % 2, True, h >= 1, h >= 2, h >= 3, 48 * ((h + 1) // 2 + 1), 64 * (h // 2) if h >= 2 else None)
            with act.Fori(2, 4) as i:
                for j in range(2):
                    a_iteration(2 * i + j, j, True, True, True, True, 48 * (i + 1 + j), 64 * i)
            for h in range(8, 11):
                a_iteration(h, h % 2, False, h < 9, h < 10, True, 48 * 5 if h == 8 else None, None)

            def mix(c, s0, n0, next_loaded, first):
                for m in range(2):
                    act.wait_ge(x_g, n0 + c + 1)
                    if not first:
                        act.wait_ge(x_mix, 2 * n0 + 2 * c - 1 + m)
                    A(sig[m][:], ps[:, m, 0:TOK], ACT.Exp, scale=-1.0).then_inc(x_e, 1)
                if next_loaded is not None:
                    for j in range(2):
                        split(j, next_loaded, (x_o if j else x_g, n0 + c + 1), MIX_COLS)

            act.wait_ge(a_comb, 16)
            mix(0, S_MIXA, 0, 48 * 6, True)
            with act.Fori(1, 3) as c:
                mix(c, S_MIXA, 0, 48 * (c + 6), False)
            mix(3, S_MIXA, 0, None, False)
            split(0, 48 * 9, (x_g, 4))

            def b_iteration(p, j, P_on, z_on, w_on, loaded):
                if w_on:
                    act.wait_ge(b_c, p - 1)
                    if not (isinstance(p, int) and p == 2):
                        act.wait_ge(b_o, p - 2)
                    A(z_w[0][:], ps[:, 4:6, 0:384], ACT.Exp)
                    A(z_w[1][:], ps[:, 6:8, 0:192], ACT.Exp).then_inc(b_w, 1)
                if P_on:
                    act.wait_ge(b_q, p + 1)
                    A(b_qT[j][:], ps[:, 0, 0:TOK], ACT.Copy, scale=0.125).then_inc(b_q_out, 1)
                if w_on:
                    act.wait_ge(b_o, p - 1)
                    A(oT_hi[:, bass.ds(p - 2, 1), :].rearrange("p a n -> p (a n)"), ps[:, 3, 0:TOK], ACT.Copy).then_inc(b_ohi, 1)
                if loaded is not None:
                    split(1 - j, loaded, (x_o, 4) if isinstance(p, int) and p == 0 else (b_vp, p),
                          MIX_COLS if isinstance(p, int) and p >= 7 else UNIT)
                if z_on:
                    act.wait_ge(b_z, p)
                    if w_on:
                        act.wait_ge(b_sp, p - 1)
                    A(z_na[0][:], ps[:, 4:6, 0:384], ACT.Abs)
                    A(z_na[1][:], ps[:, 6:8, 0:192], ACT.Abs)
                    act.drain()
                    for f in range(2):
                        A(z_na[f][:], z_na[f][:], ACT.Exp, scale=-1.0)
                    act.drain()
                    for f in range(2):
                        last = A(z_na[f][:], z_na[f][:], ACT.Ln, bias=1.0)
                    last.then_inc(b_l, 1)
                if P_on:
                    act.wait_ge(b_k, p + 1)
                    if w_on:
                        act.wait_ge(b_tk, p - 1)
                    A(b_kT[j][:, 0:TOK], ps[:, 1, 0:TOK], ACT.Copy).then_inc(b_k_out, 1)

            act.wait_ge(x_mix, 8)
            b_iteration(0, 0, True, False, False, 48 * 9)
            b_iteration(1, 1, True, True, False, 48 * 10)
            with act.Fori(1, 3) as i:
                for j in range(2):
                    b_iteration(2 * i + j, j, True, True, True, 48 * (i + 9 + j))
            b_iteration(6, 0, True, True, True, 48 * 12)
            b_iteration(7, 1, True, True, True, 48 * 13)
            b_iteration(8, 0, False, True, True, 48 * 13)
            b_iteration(9, 1, False, False, True, None)
            mix(0, S_MIXB, 4, 48 * 14, True)
            with act.Fori(1, 4) as c:
                mix(c, S_MIXB, 4, 48 * (c + 14), False)

            for s in range(2):
                act.wait_ge(gb_done, s + 1)
                A(g1b[:, s, :], ps[:, 4 + 2 * s:6 + 2 * s, :], ACT.Copy).then_inc(gb_ready, 1)
            for s in range(2):
                act.wait_ge(gb_done, s + 3)
                A(g2b[:, s, :], ps[:, 4 + 2 * s:6 + 2 * s, :], ACT.Copy).then_inc(gb_ready, 1)
            act.wait_ge(x_mix, 16)
            A(oT_hi[:], xnT[:, :, 0:TOK], ACT.Copy).then_inc(m_hi, 1)
            split(0, 48 * 18, (o_done, 3), MIX_COLS)
            split(1, 48 * 18, (o_done, 6), MIX_COLS)

            act.wait_ge(o_added, 12)
            norm_rows(xn2)
            norm_out(8)
            act.wait_ge(r_sub, 1)
            A(lsub[:], lsub[:], ACT.Exp).then_inc(r_exp, 1)
            for t in range(TILES):
                act.wait_ge(r_T, 2 * t + 1)
                A(h2tok[:, t, 0:512], ps[:, 2 + 2 * t, :], ACT.Copy).then_inc(r_rows, 1)
            act.wait_ge(r_e2, 1)
            A(e2[:], e2[:], ACT.Exp).then_inc(r_e2x, 1)

            act.wait_ge(rounds_ready, 1)
            for s in e_out_a + [e_xT, e_xT]:
                act.nop().then_inc(s, 1)
            rounds = act.value_load(rnd_i[0:1, 0:1], min_val=1, max_val=MAX_ROUNDS)

            def columns_out(x):
                q, j, n4, n2, n, e = x
                act.wait_ge(e_T[j], n2 + 2)
                act.wait_ge(e_h[j], n2 + 1)
                A(xgT[j][:], ps[:, j, :].rearrange("p (k s) -> p k s", k=KD), ACT.Copy).then_inc(e_xT, 1)

            def expo(x):
                q, j, n4, n2, n, e = x
                act.wait_ge(e_h[j], n2 + 2)
                act.wait_ge(e_hid[j], n2 + 1)
                A(h_e[j][:], ps[:, 2 + j, 0:2 * SLOTS], ACT.Exp, scale=-1.0).then_inc(e_exp, 1)

            def rows_out(x):
                q, j, n4, n2, n, e = x
                act.wait_ge(e_y[j], n2 + 3)
                act.wait_ge(y_stored[j], 16 * n2 + 16)
                A(y_sb[j][:, 0:512], ps[0:SLOTS, 4 + 2 * j, :], ACT.Copy,
                  scale=tab[:, bass.ds(e, 1), 2:3].rearrange("p a b -> p (a b)")).then_inc(e_out_a[j], 1)

            def step(r, i, u, ahead, behind):
                if ahead:
                    columns_out(at(r, i, u + 1))
                expo(at(r, i, u))
                if behind:
                    rows_out(at(r, i, u - 1))

            with act.Fori(0, rounds) as r:
                act.wait_ge(tab_in, 16 * r + 16)
                columns_out(at(r, 0, 0))
                step(r, 0, 0, True, False)
                with act.Fori(0, 7) as i:
                    for u in range(1, 5):
                        step(r, i, u, True, True)
                for u in range(29, 32):
                    step(r, 0, u, u < 31, True)
                rows_out(at(r, 0, 31))

        @block.vector
        def _(dve):
            V = nc.vector
            dve.wait_ge(c_act, 1)
            V.tensor_scalar(c_sig[64:80, :], c_sig[64:80, :], 1.0, None, ALU.add)
            dve.drain()
            V.reciprocal(c_sig[64:80, :], c_sig[64:80, :])
            dve.drain()
            V.tensor_tensor(vec_rows[64:80, :], vec_rows[64:80, :], c_sig[64:80, :], ALU.mult).then_inc(c_dve, 1)
            dve.wait_ge(vecT_done, 1)
            V.tensor_copy(vec_cols[:], ps[:, 0, 0:80])
            V.memset(c_cols[:], 0.0)
            dve.drain()
            V.tensor_copy(c_cols[:, :, 0:2], vec_cols[:, 64:80].rearrange("p (s k) -> p k s", s=2)).then_inc(vec_ready, 1)
            dve.drain()

            dve.wait_ge(rows_in, 144)
            for n in range(2):
                V.tensor_tensor(lam_prod[:, n, :], lam_rows[:, 2 * n, :], lam_rows[:, 2 * n + 1, :], ALU.mult)
            V.tensor_scalar(gqk[:, 0:2, :], gqk[:, 0:2, :], 0.125, None, ALU.mult)
            V.tensor_scalar(subln[:], subln[:], 1.0 - LAM_INIT, None, ALU.mult)
            dve.drain()
            V.tensor_reduce(lam_sum[:], lam_prod[:], AX, ALU.add).then_inc(lam_dve, 1)

            def scale_rows(dst, n0):
                dve.wait_ge(n_rstd, n0)
                for t in range(TILES):
                    V.tensor_scalar(dst[:, t, :], x_sb[:, t, :], rstd[:, t:t + 1], None, ALU.mult).then_inc(n_scaled, 1)

            def norm_out(n0):
                for k in range(1, KD, 2):
                    dve.wait_ge(n_T, n0 + k + 1)
                    V.tensor_copy(xnT[:, k, :], ps[:, 0 if k == KD - 1 else k, 0:PADDED]).then_inc(n_out_v, 1)

            def modulate(gain, shift, n0, done):
                dve.wait_ge(n_out_a, n0)
                dve.wait_ge(n_out_v, n0)
                for k in range(KD):
                    for s, sl in ((0, slice(0, SEQ)), (1, slice(SEQ, TOK))):
                        last = V.tensor_scalar(xnT[:, k, sl], xnT[:, k, sl], gain[:, k, s:s + 1],
                                               mod[:, shift + k, s:s + 1], ALU.mult, ALU.add)
                    if k % 4 == 3:
                        last.then_inc(done, 1)

            def mod_columns(lo, parts, gain, scale_at, norm_at):
                for src in parts:
                    n = int(np.prod(src.shape[1:-1]))
                    dst = mod[:, lo:lo + n, :]
                    bias = vec_cols[:, lo:lo + n].unsqueeze(2).broadcast_to([P, n, 2])
                    if len(src.shape) == 4:
                        dst, bias = (x.rearrange("p (j m) s -> p j m s", m=2) for x in (dst, bias))
                    V.tensor_tensor(dst, src, bias, ALU.add)
                    lo += n
                dve.drain()
                V.scalar_tensor_tensor(gain[:], mod[:, scale_at:scale_at + KD, :], 1.0,
                                       vec_cols[:, norm_at:norm_at + KD].unsqueeze(2).broadcast_to([P, KD, 2]),
                                       ALU.add, ALU.mult).then_inc(mod_ready, 1)
                dve.drain()

            scale_rows(xn, 1)
            dve.wait_ge(lam_act, 1)
            V.tensor_tensor(neg_lam[:], lam_exp[:, 1:2], lam_exp[:, 0:1], ALU.subtract)
            dve.drain()
            V.tensor_scalar(neg_lam[:], neg_lam[:], -LAM_INIT, None, ALU.add)
            norm_out(0)

            def split(s, j, width=UNIT):
                dve.wait_ge(split_hi, s + 1)
                V.tensor_tensor(w_lo[j][:, :, 0:width], raw[j][:, :, 0:width], f32(w_hi[j][:, :, 0:width]),
                                ALU.subtract).then_inc(split_done, 1)

            split(0, 0)
            dve.wait_ge(mod_T, 1)
            mod_columns(0, [ps[:, 5, i * 256:(i + 1) * 256].rearrange("p (m j s) -> p j m s", m=2, j=4)[:, :, :, 0:2] for i in range(2)],
                        gain1, 8, 48)
            modulate(gain1, 0, 4, h_full)
            for n in range(2):
                ks = slice(4 * n, 4 * n + 4)
                dve.wait_ge(h_hi, n + 1)
                V.tensor_tensor(hT_lo[:, ks, :], xnT[:, ks, :], f32(hT_hi[:, ks, :]), ALU.subtract).then_inc(h_ready, 1)


            def combine(parts, f):
                V.reciprocal(a_rec[:, :, parts[0][0]:parts[-1][0] + 1], a_sum[:, :, parts[0][0]:parts[-1][0] + 1])
                dve.drain()
                V.tensor_scalar(a_rec[:, 1, parts[0][0]:parts[-1][0] + 1], a_rec[:, 1, parts[0][0]:parts[-1][0] + 1],
                                neg_lam[:, 0:1], None, ALU.mult)
                for t, sl in parts:
                    V.tensor_scalar(amap[:, sl], probs[0][:, sl], a_rec[:, 0, t:t + 1], None, ALU.mult)
                dve.drain()
                for t, sl in parts:
                    last = V.scalar_tensor_tensor(amap[:, sl], probs[1][:, sl], a_rec[:, 1, t:t + 1], amap[:, sl],
                                                  ALU.mult, ALU.add)
                last.then_inc(a_comb, 1)

            def a_iteration(h, j, qk_on, s1_on, o_on, split_on):
                jq = 1 - j
                if qk_on:
                    dve.wait_ge(a_sq, h)
                    V.tensor_reduce(ss[:].rearrange("p (t n) -> p t n", t=TILES),
                                    sq[:].rearrange("p t (n c) -> p t n c", n=4), AX, ALU.add).then_inc(a_ss, 1)
                    dve.wait_ge(a_rs, h)
                    st = stage[jq][:, :, 0:256].rearrange("p t (n c) -> p t n c", n=4)
                    V.tensor_tensor(st, st, rs[:].rearrange("p (t n) -> p t n", t=TILES).unsqueeze(3).broadcast_to([P, TILES, 4, 64]),
                                    ALU.mult).then_inc(a_scaled, 1)
                if o_on:
                    dve.wait_ge(a_osq, h - 2)
                    V.tensor_reduce(o_ss[:], osq[:], AX, ALU.add).then_inc(a_oss, 1)
                    dve.wait_ge(a_ors, h - 2)
                    if not (isinstance(h, int) and h == 3):
                        dve.wait_ge(a_oT, h - 3)
                    V.tensor_tensor(o_n[:], ps[:, 7, 0:PADDED].rearrange("p (t c) -> p t c", t=TILES),
                                    o_rs[:].unsqueeze(2).broadcast_to([P, TILES, P]), ALU.mult).then_inc(a_on, 1)
                if s1_on:
                    dve.wait_ge(a_s[1], h - 1)
                    V.tensor_reduce(a_mx[:, :, 2:3], ps[:, 5:7, 0:320], AX, ALU.max)
                    dve.drain()
                    V.tensor_scalar(a_nmx[:, :, 2:3], a_mx[:, :, 2:3], -1.0, None, ALU.mult).then_inc(a_max[1], 1)
                    dve.wait_ge(a_exp[1], h - 1)
                    combine([(2, slice(384, 704))], 1)
                if o_on:
                    dve.wait_ge(a_ohi, h - 2)
                    dst = lambda x: x[:, bass.ds(h - 3, 1), :].rearrange("p a n -> p (a n)")
                    V.scalar_tensor_tensor(dst(oT_lo), ps[:, 4, 0:TOK], subln[:, 0:1], f32(dst(oT_hi)),
                                           ALU.mult, ALU.subtract).then_inc(a_olo, 1)
                if qk_on:
                    dve.wait_ge(a_qkT, h)
                    V.tensor_copy(qkT[:, 512:1024], ps[:, 4, :]).then_inc(a_qkT_dve, 1)
                if split_on:
                    split(h + 1, jq, MIX_COLS if isinstance(h, int) and h >= 7 else UNIT)
                if s1_on:
                    dve.wait_ge(a_aT, h - 1)
                    V.tensor_copy(aT[:, 512:768], ps[:, 4, 0:256]).then_inc(a_aT_dve, 1)
                if qk_on:
                    dve.wait_ge(a_s[0], h)
                    V.memset(ps[0:64, 5:7, :].rearrange("p b (u c) -> p b u c", u=2)[:, :, :, 64:128], NEG)
                    dve.drain()
                    V.tensor_reduce(a_mx[:, :, 0:1], ps[:, 5:7, 0:128], AX, ALU.max)
                    V.tensor_reduce(a_mx[:, :, 1:2], ps[:, 5:7, 128:384], AX, ALU.max)
                    dve.drain()
                    V.tensor_scalar(a_nmx[:, :, 0:2], a_mx[:, :, 0:2], -1.0, None, ALU.mult).then_inc(a_max[0], 1)
                    dve.wait_ge(a_exp[0], h)
                    combine([(0, slice(0, 128)), (1, slice(128, 384))], 0)

            dve.wait_ge(setup_done, 1)
            for h in range(4):
                a_iteration(h, h % 2, h >= 1, h >= 2, h >= 3, True)
            with dve.Fori(2, 4) as i:
                for j in range(2):
                    a_iteration(2 * i + j, j, True, True, True, True)
            for h in range(8, 11):
                a_iteration(h, h % 2, h < 9, h < 10, True, h == 8)

            def mix(c, s0, n0, split_next):
                for m in range(2):
                    n = 2 * n0 + 2 * c + m
                    dve.wait_ge(x_e, n + 1)
                    V.tensor_scalar(sig[m][:], sig[m][:], 1.0, None, ALU.add)
                    dve.drain()
                    V.reciprocal(sig_r[m][:], sig[m][:])
                if split_next:
                    split(s0 + 2 * c + 2, 0, MIX_COLS)
                dve.drain()
                dve.wait_ge(x_o, n0 + c + 1)
                for m in range(2):
                    dst = xnT[:, bass.ds(2 * c + m, 1), 0:TOK].rearrange("p a n -> p (a n)")
                    if n0:
                        V.tensor_tensor(sig_r[m][:], sig_r[m][:], ps[:, 2 + m, 0:TOK], ALU.mult)
                        dve.drain()
                        V.tensor_tensor(dst, dst, sig_r[m][:], ALU.add).then_inc(x_mix, 1)
                    else:
                        V.tensor_tensor(dst, sig_r[m][:], ps[:, 2 + m, 0:TOK], ALU.mult).then_inc(x_mix, 1)
                if split_next:
                    split(s0 + 2 * c + 3, 1, MIX_COLS)

            mix(0, S_MIXA, 0, True)
            with dve.Fori(1, 3) as c:
                mix(c, S_MIXA, 0, True)
            mix(3, S_MIXA, 0, False)
            split(S_B, 0)
            dve.wait_ge(mod_T, 2)
            mod_columns(16, [ps[:, 5 + b, :].rearrange("p (n s) -> p n s", s=32)[:, :, 0:2] for b in range(2)], gain2, 32, 56)

            def b_iteration(p, j, P_on, z_on, w_on, split_on, stored):
                jz = 1 - j
                if w_on:
                    dve.wait_ge(b_ohi, p - 1)
                    dst = lambda x: x[:, bass.ds(p - 2, 1), :].rearrange("p a n -> p (a n)")
                    V.tensor_tensor(dst(oT_lo), ps[:, 3, 0:TOK], f32(dst(oT_hi)), ALU.subtract).then_inc(b_olo, 1)
                if split_on:
                    split(S_B + p + 1, jz, MIX_COLS if isinstance(p, int) and p >= 7 else UNIT)
                if z_on:
                    dve.wait_ge(b_l, p)
                    if w_on:
                        dve.wait_ge(b_c, p - 1)
                    V.scalar_tensor_tensor(z_sp[0][:], ps[:, 4:6, 0:384], 0.0, z_na[0][:], ALU.max, ALU.add)
                    V.scalar_tensor_tensor(z_sp[1][:], ps[:, 6:8, 0:192], 0.0, z_na[1][:], ALU.max, ALU.add).then_inc(b_sp, 1)
                    dve.wait_ge(b_tk, p)
                    if stored is not None:
                        dve.wait_ge(b_stored[jz], stored)
                    V.tensor_copy(b_ktok[jz][:], ps[:, 2, 0:PADDED].rearrange("p (t c) -> p t c", t=TILES)).then_inc(b_tk_out, 1)
                    dve.wait_ge(b_tv, p)
                    if not (isinstance(p, int) and p < 3):
                        dve.wait_ge(b_o, p - 2)
                    V.tensor_copy(b_v[jz][:], ps[:, 3, 0:PADDED].rearrange("p (t c) -> p t c", t=TILES)).then_inc(b_v_out, 1)
                if P_on:
                    dve.wait_ge(b_vp, p + 1)
                    V.tensor_copy(b_vT[:, 0:TOK], ps[:, 0, 0:TOK]).then_inc(b_vT_out, 1)
                    dve.wait_ge(b_tc, p + 1)
                    V.tensor_copy(b_kT[j][:, 384:640], ps[:, 2, 0:256]).then_inc(b_tc_out, 1)

            b_iteration(0, 0, True, False, False, True, None)
            b_iteration(1, 1, True, True, False, True, None)
            b_iteration(2, 0, True, True, True, True, None)
            with dve.Fori(1, 3) as i:
                for j in range(2):
                    b_iteration(2 * i + 1 + j, 1 - j, True, True, True, True, 64 * i)
            b_iteration(7, 1, True, True, True, True, 64 * 3)
            b_iteration(8, 0, False, True, True, True, 64 * 3)
            b_iteration(9, 1, False, False, True, False, None)
            mix(0, S_MIXB, 4, True)
            with dve.Fori(1, 4) as c:
                mix(c, S_MIXB, 4, True)

            dve.wait_ge(m_hi, 1)
            V.tensor_tensor(oT_lo[:], xnT[:, :, 0:TOK], f32(oT_hi[:]), ALU.subtract).then_inc(m_ready, 1)
            for u in range(4):
                for t in range(TILES):
                    n, r = 3 * u + t, rows_of(t)
                    dve.wait_ge(o_done, n + 1)
                    dve.wait_ge(gb_ready, 2)
                    sl = slice(u * MIX_COLS, (u + 1) * MIX_COLS)
                    V.tensor_tensor(wtmp[0:r, t, :], ps[0:r, t + 3 * (u % 2), 0:MIX_COLS], g1b[0:r, t // 2, sl], ALU.mult)
                    dve.drain()
                    V.tensor_tensor(x_sb[0:r, t, sl], x_sb[0:r, t, sl], wtmp[0:r, t, :], ALU.add).then_inc(o_added, 1)
                if u < 2:
                    split(S_OUT + 2 + u, u, MIX_COLS)
            dve.drain()

            scale_rows(xn2, 2)
            norm_out(8)
            modulate(gain2, 24, 8, h2_ready)

            def bc(a, n):
                return a.unsqueeze(len(a.shape)).broadcast_to(list(a.shape) + [n])

            def row(a, n):
                return cst[:, a:a + n].unsqueeze(1).broadcast_to([P, TILES, n])

            def tt(out, a, b, op):
                ins = V.tensor_tensor(out, a, b, op)
                dve.drain()
                return ins

            def red(out, a, op):
                ins = V.tensor_reduce(out, a, AX, op)
                dve.drain()
                return ins

            dve.wait_ge(r_log, 1)
            V.tensor_copy(lg[:], ps[:, 1, 0:108].rearrange("p (t n) -> p t n", t=TILES))
            dve.drain()
            red(gmax[:], lg[:, :, 0:4], ALU.max)
            V.tensor_tensor(lsub[:], lg[:, :, 0:4], bc(gmax[:], 4), ALU.subtract).then_inc(r_sub, 1)
            tt(gtie[:], lg[:, :, 0:4], bc(gmax[:], 4), ALU.is_equal)
            tt(gtie[:], gtie[:], row(C_W4, 4), ALU.mult)
            red(gtm[:], gtie[:], ALU.max)
            tt(g1h[:], gtie[:], bc(gtm[:], 4), ALU.is_equal)
            tt(lsel4[:], lg[:, :, 4:36].rearrange("p t (g e) -> p t g e", g=GROUPS), bc(g1h[:], 8), ALU.mult)
            red(lsel[:], lsel4[:].rearrange("p t g e -> p t e g"), ALU.add)
            red(m1[:], lsel[:], ALU.max)
            tt(etie[:], lsel[:], bc(m1[:], 8), ALU.is_equal)
            tt(etie[:], etie[:], row(C_W8, 8), ALU.mult)
            red(etm[:], etie[:], ALU.max)
            tt(eh1[:], etie[:], bc(etm[:], 8), ALU.is_equal)
            V.scalar_tensor_tensor(lsel[:], eh1[:], NEG, lsel[:], ALU.mult, ALU.add)
            dve.drain()
            red(m2[:], lsel[:], ALU.max)
            tt(etie[:], lsel[:], bc(m2[:], 8), ALU.is_equal)
            tt(etie[:], etie[:], row(C_W8, 8), ALU.mult)
            red(etm[:], etie[:], ALU.max)
            tt(eh2[:], etie[:], bc(etm[:], 8), ALU.is_equal)
            V.tensor_tensor(e2[:], m2[:], m1[:], ALU.subtract).then_inc(r_e2, 1)
            for n, eh in enumerate((eh1, eh2)):
                dst = E1[n][:].rearrange("p t (g e) -> p t g e", g=GROUPS)
                V.tensor_tensor(dst, bc(g1h[:], 8), eh[:].unsqueeze(2).broadcast_to([P, TILES, GROUPS, 8]), ALU.mult)
            dve.drain()
            tt(M[:], E1[0][:], E1[1][:], ALU.add)
            V.memset(M[DEC:P, 2, :], 0.0).then_inc(r_M, 1)
            for t in range(TILES):
                dve.wait_ge(r_T, 2 * t + 2)
                V.tensor_copy(h2tok[:, t, 512:1024], ps[:, 3 + 2 * t, :]).then_inc(r_rows, 1)
            dve.wait_ge(r_exp, 1)
            red(pgsum[:], lsub[:], ALU.add)
            V.reciprocal(pg[:], pgsum[:])
            dve.wait_ge(r_e2x, 1)
            V.tensor_scalar(wsum[:], e2[:], 1.0, None, ALU.add)
            dve.drain()
            V.reciprocal(wsum[:], wsum[:])
            dve.drain()
            for n in range(2):
                V.tensor_copy(pair[n][:, :, 0:1], cst[:, C_TOK:C_TOK + 3].unsqueeze(2))
                V.tensor_scalar(pair[n][:, :, 1:2], cst[:, C_TOK:C_TOK + 3].unsqueeze(2), float(1 + n * TOK), None, ALU.add)
            V.tensor_tensor(pair[0][:, :, 2:3], pg[:].unsqueeze(2), wsum[:].unsqueeze(2), ALU.mult)
            dve.drain()
            V.tensor_tensor(pair[1][:, :, 2:3], pair[0][:, :, 2:3], e2[:].unsqueeze(2), ALU.mult)
            dve.wait_ge(r_rank, 1)
            V.scalar_tensor_tensor(rank[:], ps[:, 0, 0:96].rearrange("p (t e) -> p t e", t=TILES), float(EXPERTS),
                                   row(C_E, EXPERTS), ALU.mult, ALU.add)
            V.tensor_reduce(cnt[:], ps[:, 0, 96:128], AX, ALU.max)
            dve.drain()
            for n in range(2):
                tt(rtmp[:], E1[n][:], rank[:], ALU.mult)
                red(posf[:, n, :], rtmp[:], ALU.add)
            V.tensor_copy(posi[:], posf[:]).then_inc(r_pos, 1)
            V.tensor_scalar(thr[:], cst[:, C_THR:C_THR + MAX_ROUNDS], cnt[:, 0:1], None, ALU.is_lt)
            dve.drain()
            red(rnd[:], thr[:], ALU.add)
            V.tensor_copy(rnd_i[:], rnd[:])
            dve.drain()
            dve.nop().then_inc(rounds_ready, 1)
            for s in e_hid + e_out_v:
                dve.nop().then_inc(s, 1)
            rounds = dve.value_load(rnd_i[0:1, 0:1], min_val=1, max_val=MAX_ROUNDS)

            def swiglu(x):
                q, j, n4, n2, n, e = x
                dve.wait_ge(e_exp, n + 1)
                V.tensor_scalar(h_s[j][:], h_e[j][:], 1.0, None, ALU.add)
                dve.drain()
                V.reciprocal(h_s[j][:], h_s[j][:])
                dve.drain()
                V.tensor_tensor(h_s[j][:], h_s[j][:], ps[:, 2 + j, 0:2 * SLOTS], ALU.mult)
                dve.drain()
                dve.wait_ge(e_y[j], n2 + 2)
                V.tensor_tensor(hid[j][:].rearrange("p m s -> p (m s)"), h_s[j][:],
                                ps[:, 2 + j, 2 * SLOTS:4 * SLOTS], ALU.mult).then_inc(e_hid[j], 1)

            def rows_out(x):
                q, j, n4, n2, n, e = x
                dve.wait_ge(e_y[j], n2 + 3)
                dve.wait_ge(y_stored[j], 16 * n2 + 16)
                V.tensor_scalar(y_sb[j][:, 512:1024], ps[0:SLOTS, 5 + 2 * j, :],
                                tab[:, bass.ds(e, 1), 2:3].rearrange("p a b -> p (a b)"), None, ALU.mult).then_inc(e_out_v[j], 1)

            with dve.Fori(0, rounds) as r:
                dve.wait_ge(tab_in, 16 * r + 16)
                V.tensor_copy(tab_i[:], tab[:, :, 0:2]).then_inc(tab_ready, 1)
                swiglu(at(r, 0, 0))
                with dve.Fori(0, 7) as i:
                    for u in range(1, 5):
                        swiglu(at(r, i, u))
                        rows_out(at(r, i, u - 1))
                for u in range(29, 32):
                    swiglu(at(r, 0, u))
                    rows_out(at(r, 0, u - 1))
                rows_out(at(r, 0, 31))

            dve.wait_ge(back, 64)
            for t in range(TILES):
                r = rows_of(t)
                V.tensor_tensor(ya[0:r, t, :], ya[0:r, t, :], yb[0:r, t, :], ALU.add)
            dve.drain()
            for t in range(TILES):
                r = rows_of(t)
                V.tensor_tensor(ya[0:r, t, :], ya[0:r, t, :], g2b[0:r, t // 2, :], ALU.mult)
            dve.drain()
            for t in range(TILES):
                r = rows_of(t)
                V.tensor_tensor(x_sb[0:r, t, :], x_sb[0:r, t, :], ya[0:r, t, :], ALU.add)
            dve.drain()
            dve.nop().then_inc(y_done, 2)

        @block.gpsimd
        def _(pool):
            G = nc.gpsimd
            G.memset(zero[:], 0.0).then_inc(zero_ready, 1)
            G.memset(ones[:], 1.0)
            G.memset(ones_neg[:], -1.0)
            G.memset(eps[:], EPS)
            pool.drain()
            G.memset(x_sb[DEC:P, 2, :], 0.0)
            pool.drain()
            G.memset(amap[:, 704:768], 0.0)
            pool.drain()
            pool.nop().then_inc(setup_done, 1)

            def rope(m, j, v_free):
                pool.wait_ge(a_scaled, m + 1)
                st = stage[j]
                G.tensor_tensor(st[:, :, 0:256], st[:, :, 0:256],
                                gqk[:].rearrange("p n c -> p (n c)").unsqueeze(1).broadcast_to([P, TILES, 256]), ALU.mult)
                pool.drain()
                x16 = st[:, :, 0:256].rearrange("p t (n c) -> p t n c", n=4)[:, :, :, 0:16]
                cos = cst[:, C_ROPEC:C_ROPEC + 48].rearrange("p (t c) -> p t c", t=TILES)
                sin = cst[:, C_ROPES:C_ROPES + 48].rearrange("p (t c) -> p t c", t=TILES)

                def over_heads(a, lo, hi):
                    return a[:, :, lo:hi].unsqueeze(2).broadcast_to([P, TILES, 4, hi - lo])

                G.tensor_tensor(rope_x[:], x16, over_heads(cos, 0, 16), ALU.mult)
                G.tensor_tensor(rope_y[:, :, :, 0:8], x16[:, :, :, 8:16], over_heads(sin, 0, 8), ALU.mult)
                G.tensor_tensor(rope_y[:, :, :, 8:16], x16[:, :, :, 0:8], over_heads(sin, 8, 16), ALU.mult)
                pool.drain()
                G.tensor_tensor(x16, rope_x[:], rope_y[:], ALU.add).then_inc(a_roped, 1)
                if v_free is not None:
                    before = pool.to_reg(v_free)
                    pool.wait_ge(setup_done, 1)
                    pool.wait_ge(a_pv, before)
                G.tensor_copy(v_keep[j][:], st[:, :, 256:384]).then_inc(a_vkept, 1)
                pool.drain()

            for m in range(2):
                rope(m, m, None)
            with pool.Fori(1, 4) as i:
                for j in range(2):
                    rope(2 * i + j, j, 2 * i + j - 1)

            pool.wait_ge(a_olo, 8)
            pool.wait_ge(x_mix, 8)
            for j in range(2):
                G.memset(b_kT[j][:, TOK:PADDED], 0.0)
            G.memset(b_vT[:, TOK:PADDED], 0.0)
            pool.drain()
            pool.nop().then_inc(b_zero, 1)

            def causal(bufs, done):
                for hh in range(2):
                    blocks = bufs[0][:, hh, :].rearrange("p (u c) -> p u c", c=P)[:, 0:3:2, :]
                    G.affine_select(out=blocks, in_=blocks, pattern=[[0, 2], [1, P]], compare_op=ALU.is_gt, fill=0.0,
                                    base=0, channel_multiplier=-1)
                blocks = bufs[1][:, :, P:P + DEC]
                G.affine_select(out=blocks, in_=blocks, pattern=[[0, 2], [1, DEC]], compare_op=ALU.is_gt, fill=0.0,
                                base=0, channel_multiplier=-1).then_inc(done, 1)

            pool.wait_ge(b_sp, 1)
            causal(z_sp, b_spm)
            with pool.Fori(1, 8) as m:
                pool.wait_ge(setup_done, 1)
                pool.wait_ge(b_w, m)
                causal(z_w, b_wm)
                logits = pool.to_reg(m + 1)
                pool.wait_ge(setup_done, 1)
                pool.wait_ge(b_sp, logits)
                causal(z_sp, b_spm)
            pool.wait_ge(b_w, 8)
            causal(z_w, b_wm)

            pool.wait_ge(r_rows, 6)
            for j, ts in enumerate((slice(0, 2), slice(2, 3))):
                pool.dma_start(h2_dram.rearrange("(t p) d -> p t d", p=P)[:, ts, :], h2tok[:, ts, :]).then_inc(y_stored[j], 16)
            pool.wait_ge(r_pos, 1)
            pool.wait_ge(tab_zero, 16)
            for n in range(2):
                for t in range(TILES):
                    r = rows_of(t)
                    G.indirect_dma_start(tab_dram, bass.IndirectOffsetOnAxis(ap=posi[0:r, n, t:t + 1], axis=0),
                                         pair[n][0:r, t, :], None).then_inc(tab_put, 16)
            pool.wait_ge(tab_put, 96)
            for j in range(2):
                pool.wait_ge(y_stored[j], 16)
            pool.wait_ge(rounds_ready, 1)
            rounds = pool.value_load(rnd_i[0:1, 0:1], min_val=1, max_val=MAX_ROUNDS)

            def counts(n4):
                plain = [pool.to_reg(2 * n4 + n) for n in range(1, 6)]
                stores = [pool.to_reg(32 * n4 + 16 * n) for n in range(1, 4)]
                return plain, stores

            def gather(q, copied, transposed, e):
                pool.wait_ge(setup_done, 1)
                pool.wait_ge(e_T[q % 2], transposed)
                G.tensor_copy(idx[q][:], tab_i[:, bass.ds(e, 1), 0:1].rearrange("p a b -> p (a b)")).then_inc(idx_ready[q % 2], 1)
                pool.wait_ge(setup_done, 1)
                pool.wait_ge(idx_ready[q % 2], copied)
                G.indirect_dma_start(xg[q][:], None, h2_dram, bass.IndirectOffsetOnAxis(ap=idx[q][:, 0:1], axis=0)).then_inc(gathered[q], 16)

            def scatter(q, plain, stores, e):
                j, h = q % 2, q // 2
                pool.wait_ge(setup_done, 1)
                pool.wait_ge(e_out_a[j], plain[h + 1])
                pool.wait_ge(e_out_v[j], plain[h + 1])
                G.tensor_copy(row_idx[j][:], tab_i[:, bass.ds(e, 1), 1:2].rearrange("p a b -> p (a b)")).then_inc(row_ready[j], 1)
                pool.wait_ge(setup_done, 1)
                pool.wait_ge(row_ready[j], plain[h])
                pool.wait_ge(y_stored[1 - j], stores[h + j])
                G.indirect_dma_start(y_dram, bass.IndirectOffsetOnAxis(ap=row_idx[j][:, 0:1], axis=0), y_sb[j][:], None).then_inc(y_stored[j], 16)

            with pool.Fori(0, rounds) as r:
                for j in range(2):
                    pool.wait_ge(y_stored[j], 256 * r + 16)
                pool.dma_start(tab[:], tab_dram.rearrange("(s e) a -> s e a", e=EXPERTS)[bass.ds(r * SLOTS, SLOTS)]).then_inc(tab_in, 16)
                after, plain = pool.to_reg(r + 1), [pool.to_reg(16 * r + n) for n in range(1, 4)]
                pool.wait_ge(setup_done, 1)
                pool.wait_ge(tab_ready, after)
                for e in range(6):
                    gather(e % 4, plain[e // 2], plain[e // 4], e)
                for v in [after] + plain:
                    pool.free_register(v)

                def scatter_and_gather(i, qs):
                    plain, stores = counts(8 * r + i)
                    for q in qs:
                        scatter(q, plain, stores, 4 * i + q)
                        gather((q + 2) % 4, plain[q // 2 + 3], plain[q // 2 + 2], 4 * i + q + 6)
                    for v in plain + stores:
                        pool.free_register(v)

                with pool.Fori(0, 6) as i:
                    scatter_and_gather(i, range(4))
                scatter_and_gather(6, range(2))
                for i, qs in ((6, (2, 3)), (7, range(4))):
                    plain, stores = counts(8 * r + i)
                    for q in qs:
                        scatter(q, plain, stores, 4 * i + q)
                    for v in plain + stores:
                        pool.free_register(v)
            stored_rows = pool.to_reg(256 * rounds + 16)
            pool.wait_ge(setup_done, 1)
            for j in range(2):
                pool.wait_ge(y_stored[j], stored_rows)
            for n, dst in enumerate((ya, yb)):
                first = 1 + n * TOK
                pool.dma_start(dst[:, 0:2, :], y_dram[first:first + SEQ].rearrange("(t p) d -> p t d", p=P)).then_inc(back, 16)
                pool.dma_start(dst[0:DEC, 2, :], y_dram[first + SEQ:first + TOK]).then_inc(back, 16)



_SHAPES = (("y_prompt", (1, SEQ, D)), ("y_sample", (1, DEC, D)),
           ("a_k_prompt", (1, 1, SEQ, 16, 64)), ("a_v_prompt", (1, 1, SEQ, 8, 128)),
           ("b_k_prompt", (1, 1, SEQ, 16, 64)), ("b_v_prompt", (1, 1, SEQ, 16, 64)),
           ("a_k_sample", (1, 1, DEC, 16, 64)), ("a_v_sample", (1, 1, DEC, 8, 128)),
           ("b_k_sample", (1, 1, DEC, 16, 64)), ("b_v_sample", (1, 1, DEC, 16, 64)))


def kernel(**inputs):
    import concourse.bacc as bacc
    from concourse.bass_utils import run_bass_kernel_spmd

    nc = bacc.Bacc("TRN2", target_bir_lowering=False, num_devices=1)
    arrays = {"shape_constants": shape_constants()}
    for name, a in inputs.items():
        a = np.ascontiguousarray(a)
        if name.startswith("cache"):
            a = a.reshape(PAST, D)
        elif not name.startswith(("x_", "c_")):
            a = a.reshape(a.shape[1:])
        arrays[name] = a
    t_in = {name: nc.dram_tensor("in_" + name, a.shape, mybir.dt.from_np(a.dtype), kind="ExternalInput").ap()
            for name, a in arrays.items()}
    t_out = {name: nc.dram_tensor("out_" + name, (shape[-3] * shape[-2] * shape[-1] // D, D) if len(shape) == 5 else shape[1:],
                                  F32, kind="ExternalOutput").ap() for name, shape in _SHAPES}
    build(nc, t_in, t_out)
    r = run_bass_kernel_spmd(nc, [{"in_" + n: a for n, a in arrays.items()}], core_ids=[0])
    return tuple(np.asarray(r.results[0]["out_" + name]).reshape(shape) for name, shape in _SHAPES)
```
